# Optimizing a Trainium2 kernel written in Bass

```python
import jax, jax.numpy as jnp
from jax import lax
import numpy as np

D_MODEL = 1024
BATCH = 1
SEQ = 512
DEPTH = 1
DEC_BATCH = 8
DEC_SEQ = 4
PAST_LEN = 4096
PAGE_SIZE = 128

SB_HEADS = 8
SB_HEAD_DIM = 64
SB_WIDTH = SB_HEADS * SB_HEAD_DIM
Q_BLOCK = 128
SB_BIAS_START = -2.0
RET_HEADS = 4
RET_QK_DIM = 128
RET_V_DIM = 256
RET_QK_WIDTH = RET_HEADS * RET_QK_DIM
RET_V_WIDTH = RET_HEADS * RET_V_DIM
RET_CHUNK = 128
ROPE_BASE = 10000.0
PEER_HEADS = 8
PEER_HALF = 128
PEER_QUERY_DIM = 2 * PEER_HALF
N_KEYS = 128
N_EXPERTS = N_KEYS * N_KEYS
PEER_TOPK = 16
PLE_DIM = 256
RMS_EPS = 1e-6

PROJ_SIZES = (SB_WIDTH, SB_WIDTH, SB_WIDTH, RET_QK_WIDTH, RET_QK_WIDTH, RET_V_WIDTH, RET_V_WIDTH, D_MODEL, D_MODEL)
PROJ_SPLITS = tuple(int(s) for s in np.cumsum(PROJ_SIZES)[:-1])
PROJ_WIDTH = int(sum(PROJ_SIZES))

kernel_name = "stickbreak_retention_peer_hybrid_step"

F32 = jnp.float32

def rms_norm(x, g):
    xf = x.astype(F32)
    y = xf * lax.rsqrt(jnp.mean(xf * xf, axis=-1, keepdims=True) + RMS_EPS)
    return (y * g.astype(F32)).astype(x.dtype)

def rotary(x, pos):
    half = x.shape[-1] // 2
    inv = ROPE_BASE ** (-jnp.arange(half, dtype=F32) / half)
    ang = pos.astype(F32)[:, None] * inv[None, :]
    cos = jnp.cos(ang)[None, :, None, :]
    sin = jnp.sin(ang)[None, :, None, :]
    xf = x.astype(F32)
    x1, x2 = xf[..., :half], xf[..., half:]
    return jnp.concatenate([x1 * cos - x2 * sin, x1 * sin + x2 * cos], axis=-1).astype(x.dtype)

def ret_log_gamma():
    return jnp.log1p(-jnp.exp2(-5.0 - jnp.arange(RET_HEADS, dtype=F32)))

def mixer_inputs(x, pos, norm_g, w_in, q_g, k_g):
    B, T, _ = x.shape
    h = rms_norm(x, norm_g)
    proj = h @ w_in
    qa, ka, va, qb, kb, vb, gb, ga_pre, gb_pre = jnp.split(proj, PROJ_SPLITS, axis=-1)
    qa = rms_norm(qa.reshape(B, T, SB_HEADS, SB_HEAD_DIM), q_g)
    ka = rms_norm(ka.reshape(B, T, SB_HEADS, SB_HEAD_DIM), k_g)
    va = va.reshape(B, T, SB_HEADS, SB_HEAD_DIM)
    qb = rotary(qb.reshape(B, T, RET_HEADS, RET_QK_DIM), pos)
    kb = rotary(kb.reshape(B, T, RET_HEADS, RET_QK_DIM), pos) * (RET_QK_DIM ** -0.5)
    vb = vb.reshape(B, T, RET_HEADS, RET_V_DIM)
    return qa, ka, va, qb, kb, vb, gb, ga_pre, gb_pre

def sb_attend(q, k, v, q_pos, k_pos, bias):
    z = jnp.einsum('bqhd,bkhd->bhqk', q.astype(F32), k.astype(F32)) * (q.shape[-1] ** -0.5)
    z = z + bias.astype(F32)[None, :, None, None]
    mask = k_pos[None, :] < q_pos[:, None]
    log_not = jnp.where(mask, jax.nn.log_sigmoid(-z), 0.0)
    suffix = lax.cumsum(log_not, axis=3, reverse=True) - log_not
    a = jnp.where(mask, jnp.exp(jax.nn.log_sigmoid(z) + suffix), 0.0)
    return jnp.einsum('bhqk,bkhd->bqhd', a, v.astype(F32))

def sb_prompt(q, k, v, bias):
    B, S, H, D = q.shape
    nb = S // Q_BLOCK
    qb = q.reshape(B, nb, Q_BLOCK, H, D).transpose(1, 0, 2, 3, 4)
    posb = jnp.arange(S).reshape(nb, Q_BLOCK)
    k_pos = jnp.arange(S)
    out = lax.map(lambda a: sb_attend(a[0], k, v, a[1], k_pos, bias), (qb, posb))
    return out.transpose(1, 0, 2, 3, 4).reshape(B, S, H, D)

def retention_chunk(state, q, k, v):
    C = q.shape[1]
    lg = ret_log_gamma()
    idx = jnp.arange(C, dtype=F32)
    diff = idx[:, None] - idx[None, :]
    causal = diff >= 0
    decay = jnp.where(causal[None], jnp.exp(jnp.where(causal, diff, 0.0)[None] * lg[:, None, None]), 0.0)
    qf, kf, vf = q.astype(F32), k.astype(F32), v.astype(F32)
    scores = jnp.einsum('bihd,bjhd->bhij', qf, kf) * decay[None]
    inner = jnp.einsum('bhij,bjhe->bihe', scores, vf)
    q_decay = jnp.exp((idx[:, None] + 1.0) * lg[None, :])
    cross = jnp.einsum('bihd,bhde->bihe', qf, state) * q_decay[None, :, :, None]
    k_decay = jnp.exp((C - 1.0 - idx)[:, None] * lg[None, :])
    new_state = jnp.exp(C * lg)[None, :, None, None] * state + jnp.einsum('bjhd,bjhe->bhde', kf * k_decay[None, :, :, None], vf)
    return new_state, inner + cross

def retention_prompt(q, k, v):
    B, S, H, DK = q.shape
    nc = S // RET_CHUNK
    to_chunks = lambda t: t.reshape(B, nc, RET_CHUNK, H, t.shape[-1]).transpose(1, 0, 2, 3, 4)
    init = jnp.zeros((B, H, DK, v.shape[-1]), F32)
    final, outs = lax.scan(lambda s, xs: retention_chunk(s, *xs), init, (to_chunks(q), to_chunks(k), to_chunks(v)))
    return final, outs.transpose(1, 0, 2, 3, 4).reshape(B, S, H, v.shape[-1])

def peer_block(h, w_q, sub_keys, u_tab, v_tab):
    T = h.shape[0]
    q = (h @ w_q).reshape(T, PEER_HEADS, 2, PEER_HALF)
    s = jnp.einsum('thcd,hcnd->thcn', q.astype(F32), sub_keys.astype(F32))
    s1, i1 = lax.top_k(s[:, :, 0], PEER_TOPK)
    s2, i2 = lax.top_k(s[:, :, 1], PEER_TOPK)
    cand = (s1[..., :, None] + s2[..., None, :]).reshape(T, PEER_HEADS, PEER_TOPK * PEER_TOPK)
    top, flat = lax.top_k(cand, PEER_TOPK)
    e = jnp.take_along_axis(i1, flat // PEER_TOPK, axis=-1) * N_KEYS + jnp.take_along_axis(i2, flat % PEER_TOPK, axis=-1)
    g = jax.nn.softmax(top, axis=-1)
    u = u_tab[e]
    act = jax.nn.gelu(jnp.einsum('thkd,td->thk', u, h).astype(F32))
    return jnp.einsum('thk,thkd->td', (g * act).astype(h.dtype), v_tab[e])

def peer_apply(h, block, w_q, sub_keys, u_tab, v_tab):
    B, T, D = h.shape
    hb = h.reshape(-1, block, D)
    out = lax.map(lambda t: peer_block(t, w_q, sub_keys, u_tab, v_tab), hb)
    return out.reshape(B, T, D)

def merge_and_channel(x, o_a, o_b, gb, ga_pre, gb_pre, p_emb, block, ret_norm_g, w_a_up, w_b_up, w_out,
                      norm_ffn_g, peer_w_q, peer_sub_keys, peer_u, peer_v, norm_ple_g, w_ple_gate, w_ple):
    B, T, _ = x.shape
    y_a = o_a.astype(x.dtype).reshape(B, T, SB_WIDTH) @ w_a_up
    ob = rms_norm(o_b, ret_norm_g).astype(x.dtype) * jax.nn.silu(gb.reshape(B, T, RET_HEADS, RET_V_DIM))
    y_b = ob.reshape(B, T, RET_V_WIDTH) @ w_b_up
    merged = jax.nn.sigmoid(ga_pre) * y_a + jax.nn.sigmoid(gb_pre) * y_b
    x = x + merged @ w_out
    h2 = rms_norm(x, norm_ffn_g)
    x = x + peer_apply(h2, block, peer_w_q, peer_sub_keys, peer_u, peer_v)
    gate = jax.nn.sigmoid(rms_norm(x, norm_ple_g) @ w_ple_gate)
    return x + gate * (p_emb @ w_ple)

def setup_inputs(seed: int = 0) -> dict:
    key = jax.random.key(seed)
    ks = jax.random.split(key, 32)
    n_pages = PAST_LEN // PAGE_SIZE
    n_used = DEC_BATCH * n_pages
    n_phys = n_used + max(1, n_used // 4)
    nrm = lambda k, shape, scale: jax.random.normal(k, shape, F32) * scale
    gain = lambda k, shape: 1.0 + 0.02 * jax.random.normal(k, shape, F32)
    page_table = jax.random.permutation(ks[7], n_phys)[:n_used].reshape(DEC_BATCH, n_pages).astype(jnp.int32)
    sb_bias = (SB_BIAS_START - jnp.arange(SB_HEADS, dtype=F32))[None, :] + 0.1 * jax.random.normal(ks[24], (DEPTH, SB_HEADS), F32)
    return {
        "x_prompt": nrm(ks[0], (BATCH, SEQ, D_MODEL), 1.0),
        "x_sample": nrm(ks[1], (DEC_BATCH, DEC_SEQ, D_MODEL), 1.0),
        "cache_k": nrm(ks[2], (DEPTH, n_phys, PAGE_SIZE, SB_HEADS, SB_HEAD_DIM), 1.0),
        "cache_v": nrm(ks[3], (DEPTH, n_phys, PAGE_SIZE, SB_HEADS, SB_HEAD_DIM), 1.0),
        "state_ret": nrm(ks[4], (DEPTH, DEC_BATCH, RET_HEADS, RET_QK_DIM, RET_V_DIM), 0.5),
        "page_table": page_table,
        "p_prompt": nrm(ks[5], (DEPTH, BATCH, SEQ, PLE_DIM), 1.0),
        "p_sample": nrm(ks[6], (DEPTH, DEC_BATCH, DEC_SEQ, PLE_DIM), 1.0),
        "norm_mix_g": gain(ks[8], (DEPTH, D_MODEL)),
        "w_in": nrm(ks[9], (DEPTH, D_MODEL, PROJ_WIDTH), D_MODEL ** -0.5),
        "q_norm_g": gain(ks[10], (DEPTH, SB_HEAD_DIM)),
        "k_norm_g": gain(ks[11], (DEPTH, SB_HEAD_DIM)),
        "sb_bias": sb_bias,
        "ret_norm_g": gain(ks[12], (DEPTH, RET_HEADS, RET_V_DIM)),
        "w_a_up": nrm(ks[13], (DEPTH, SB_WIDTH, D_MODEL), SB_WIDTH ** -0.5),
        "w_b_up": nrm(ks[14], (DEPTH, RET_V_WIDTH, D_MODEL), RET_V_WIDTH ** -0.5),
        "w_out": nrm(ks[15], (DEPTH, D_MODEL, D_MODEL), D_MODEL ** -0.5),
        "norm_ffn_g": gain(ks[16], (DEPTH, D_MODEL)),
        "peer_w_q": nrm(ks[17], (DEPTH, D_MODEL, PEER_HEADS * PEER_QUERY_DIM), D_MODEL ** -0.5),
        "peer_sub_keys": nrm(ks[18], (DEPTH, PEER_HEADS, 2, N_KEYS, PEER_HALF), PEER_HALF ** -0.5),
        "peer_u": nrm(ks[19], (DEPTH, N_EXPERTS, D_MODEL), D_MODEL ** -0.5),
        "peer_v": nrm(ks[20], (DEPTH, N_EXPERTS, D_MODEL), PEER_HEADS ** -0.5),
        "norm_ple_g": gain(ks[21], (DEPTH, D_MODEL)),
        "w_ple_gate": nrm(ks[22], (DEPTH, D_MODEL, D_MODEL), D_MODEL ** -0.5),
        "w_ple": nrm(ks[23], (DEPTH, PLE_DIM, D_MODEL), PLE_DIM ** -0.5),
    }

def reference(x_prompt, x_sample, cache_k, cache_v, state_ret, page_table, p_prompt, p_sample,
              norm_mix_g, w_in, q_norm_g, k_norm_g, sb_bias, ret_norm_g, w_a_up, w_b_up, w_out, norm_ffn_g,
              peer_w_q, peer_sub_keys, peer_u, peer_v, norm_ple_g, w_ple_gate, w_ple):
    S = x_prompt.shape[1]
    DB, T = x_sample.shape[0], x_sample.shape[1]
    past_len = page_table.shape[1] * cache_k.shape[2]
    pos_p = jnp.arange(S)
    pos_s = past_len + jnp.arange(T)
    k_pos_s = jnp.arange(past_len + T)
    xp, xs = x_prompt, x_sample
    kp, vp, sp, kn, vn, sn = [], [], [], [], [], []
    for i in range(DEPTH):
        tail = (ret_norm_g[i], w_a_up[i], w_b_up[i], w_out[i], norm_ffn_g[i], peer_w_q[i], peer_sub_keys[i],
                peer_u[i], peer_v[i], norm_ple_g[i], w_ple_gate[i], w_ple[i])
        qa, ka, va, qb, kb, vb, gb, ga_pre, gb_pre = mixer_inputs(xp, pos_p, norm_mix_g[i], w_in[i], q_norm_g[i], k_norm_g[i])
        o_a = sb_prompt(qa, ka, va, sb_bias[i])
        st_p, o_b = retention_prompt(qb, kb, vb)
        xp = merge_and_channel(xp, o_a, o_b, gb, ga_pre, gb_pre, p_prompt[i], Q_BLOCK, *tail)
        kp.append(ka.astype(cache_k.dtype))
        vp.append(va.astype(cache_v.dtype))
        sp.append(st_p.astype(state_ret.dtype))
        qa, ka, va, qb, kb, vb, gb, ga_pre, gb_pre = mixer_inputs(xs, pos_s, norm_mix_g[i], w_in[i], q_norm_g[i], k_norm_g[i])
        k_past = cache_k[i][page_table].reshape(DB, past_len, SB_HEADS, SB_HEAD_DIM)
        v_past = cache_v[i][page_table].reshape(DB, past_len, SB_HEADS, SB_HEAD_DIM)
        k_all = jnp.concatenate([k_past, ka.astype(k_past.dtype)], axis=1)
        v_all = jnp.concatenate([v_past, va.astype(v_past.dtype)], axis=1)
        o_a = sb_attend(qa, k_all, v_all, pos_s, k_pos_s, sb_bias[i])
        st_s, o_b = retention_chunk(state_ret[i].astype(F32), qb, kb, vb)
        xs = merge_and_channel(xs, o_a, o_b, gb, ga_pre, gb_pre, p_sample[i], T, *tail)
        kn.append(ka.astype(cache_k.dtype))
        vn.append(va.astype(cache_v.dtype))
        sn.append(st_s.astype(state_ret.dtype))
    return (xp, xs, jnp.stack(kp), jnp.stack(vp), jnp.stack(sp), jnp.stack(kn), jnp.stack(vn), jnp.stack(sn))


_drawn_inputs = setup_inputs


def setup_inputs(seed=0):
    import zlib

    import numpy as np

    out = dict(_drawn_inputs(seed))
    spreads = {}
    factors = {'q_norm_g': 19.594,
     'k_norm_g': 7.474,
     'ret_norm_g': 10.69,
     'norm_ple_g': 200.0,
     'norm_ffn_g': 9.499}
    for name, (base, spread) in spreads.items():
        noise = np.random.default_rng([zlib.crc32(name.encode()), seed]).standard_normal(out[name].shape)
        drawn = base * np.exp(spread * noise) if base else spread * noise
        out[name] = __import__('jax').numpy.asarray(drawn.astype(out[name].dtype))
    for name, factor in factors.items():
        out[name] = (out[name] * factor).astype(out[name].dtype)
    return out
```

```python
from contextlib import ExitStack

import concourse.bass as bass
from concourse import mybir

F32 = mybir.dt.float32
I32 = mybir.dt.int32
U32 = mybir.dt.uint32
ALU = mybir.AluOpType
ACT = mybir.ActivationFunctionType
AX = mybir.AxisListType

P = 128
D = 1024
DC = D // P
SEQ = 512
PT = SEQ // P
DECB, DECT = 8, 4
NS = DECB * DECT
TILES = PT + 1
TOK = SEQ + NS
H, HD = 8, 64
HP = H // 2
RH, RK, RV = 4, 128, 256
PAGES = 32
PEER_H, TOPK, NKEY = 8, 16, 128
PLE = 256
EPS = 1e-6
FAR = -1.0e30
GONE = -3.0e38
GELU_A, GELU_C = 0.044715, 0.7978845608028654
PAST = PAGES * P

SLOTS = PT * PEER_H + 2


def rows(t):
    return P if t < PT else NS


def cols(t):
    return slice(t * P, t * P + rows(t))


def const_layout():
    sizes = dict(ident=128, tri=128, ones=512, diag_mask=128, decay=RH * 128, q_decay=RH * 128,
                 k_decay=RH, s_decay=RH * NS, s_q_decay=RH * NS, s_block=DECB * NS,
                 s_k_decay=DECB * RH, carry_in=128, carry_all=128, spread=128, select=32,
                 new_mask=DECB * NS, cos=TILES * 64, sin=TILES * 128, iota=16, gather4=32,
                 eps=1)
    at, out = 0, {}
    for name, n in sizes.items():
        out[name] = (at, n)
        at += n
    return out, at


CONST_AT, CONST_N = const_layout()


def gammas():
    import math
    return [math.log1p(-(2.0 ** (-5.0 - h))) for h in range(RH)]


def const_array():
    import numpy as np
    c = {n: np.zeros((P, k), np.float32) for n, (_, k) in CONST_AT.items()}
    p = np.arange(P)
    c["ident"][:] = np.eye(P)
    c["tri"][:] = p[:, None] >= p[None, :]
    c["ones"][:] = 1.0
    c["diag_mask"][:] = np.where(p[:, None] < p[None, :], 3.0e38, FAR)
    lg = np.array(gammas())
    dif = p[None, :] - p[:, None]
    for h in range(RH):
        c["decay"][:, h * P:(h + 1) * P] = np.where(dif >= 0, np.exp(np.maximum(dif, 0) * lg[h]), 0)
        c["q_decay"][:, h * P:(h + 1) * P] = np.exp((p[None, :] + 1) * lg[h])
        c["k_decay"][:, h] = np.exp((P - 1 - p) * lg[h])
    s = np.arange(NS)
    same = (s[:, None] // DECT) == (s[None, :] // DECT)
    sd = s[None, :] - s[:, None]
    for h in range(RH):
        c["s_decay"][:NS, h * NS:(h + 1) * NS] = np.where(same & (sd >= 0), np.exp(np.maximum(sd, 0) * lg[h]), 0)
        c["s_q_decay"][:, h * NS:(h + 1) * NS] = np.exp((s % DECT + 1) * lg[h])[None, :]
    for b in range(DECB):
        c["s_block"][:, b * NS:(b + 1) * NS] = (s // DECT == b)[None, :]
        for h in range(RH):
            c["s_k_decay"][:NS, b * RH + h] = np.where(s // DECT == b, np.exp((DECT - 1 - s % DECT) * lg[h]), 0)
        c["new_mask"][:NS, b * NS:(b + 1) * NS] = np.where(
            (s[None, :] // DECT == b) & (s[None, :] % DECT < s[:, None] % DECT), 3.0e38, FAR)
    same32 = (p[:, None] % 32) == (p[None, :] % 32)
    c["carry_in"][:] = same32 & (p[:, None] // 32 > p[None, :] // 32)
    c["carry_all"][:] = same32
    c["spread"][:] = same32 & (p[:, None] < 32)
    c["select"][:] = (p[:, None] % 32) == np.arange(32)[None, :]
    c["gather4"][:] = c["select"]
    c["iota"][:] = np.arange(16)[None, :]
    c["eps"][:] = EPS
    half = RK // 2
    inv = (np.float32(10000.0) ** (-np.arange(half, dtype=np.float32) / np.float32(half))).astype(np.float32)
    for t in range(TILES):
        pos = (t * P + p if t < PT else PAST + p % DECT).astype(np.float32)
        ang = pos[:, None] * inv[None, :]
        c["cos"][:, t * 64:(t + 1) * 64] = np.cos(ang)
        c["sin"][:, t * 128:t * 128 + 64] = -np.sin(ang)
        c["sin"][:, t * 128 + 64:(t + 1) * 128] = np.sin(ang)
    return np.concatenate([c[n] for n in CONST_AT], axis=1)


W_AT = 5120
W_SIZE = DC * 512
W_BUFS = 3
HT_AT = W_AT + W_BUFS * W_SIZE
OAT_AT = HT_AT + DC * TOK
R = OAT_AT + HP * TOK
ARENA = R + 28800


def bass_decoder_step(nc, ins, outs, consts):
    ctx = ExitStack()
    with ctx:
        arena = ctx.enter_context(nc.sbuf_tensor("arena", [P, ARENA], F32))
        ps = ctx.enter_context(nc.psum_tensor("ps", [P, 8, 512], F32))

        def sem(name):
            return ctx.enter_context(nc.semaphore(name))

        def mem(at, *shape, parts=P, first=0):
            n = 1
            for k in shape:
                n *= k
            v = arena[first:first + parts, at:at + n]
            if len(shape) == 1:
                return v
            names = "abcd"[:len(shape)]
            pattern = "p (" + " ".join(names) + ") -> p " + " ".join(names)
            return v.rearrange(pattern, **dict(zip(names, shape)))

        def const(name, *shape):
            at, n = CONST_AT[name]
            return mem(at, *(shape or (n,)))

        def bcast(ap, *shape):
            return ap.to_broadcast([*shape])

        ident = const("ident")
        at = CONST_N
        def param(n):
            nonlocal at
            at += n
            assert at <= W_AT
            return at - n
        qk_gain = mem(param(2 * HD), 2, HD)
        mix_gain = mem(param(DC), DC)
        ple_gain = mem(param(DC), DC)
        bias_row = mem(param(H), H)
        bias_col = mem(param(1), 1)
        stat = mem(param(64), 64)
        stat2 = mem(param(64), 64)
        SMALL2_AT = at
        table = ctx.enter_context(nc.sbuf_tensor("table", [1, DECB * PAGES], I32))

        wbuf = [mem(W_AT + k * W_SIZE, DC, 512) for k in range(W_BUFS)]
        hT = mem(HT_AT, DC, TOK)
        oaT = mem(OAT_AT, HP, TOK)

        w_in = ins["w_in"]
        W_IN = dict(qa=0, ka=1, va=2, qb=3, kb=4, vb0=5, vb1=6, gb0=7, gb1=8, ga0=9, ga1=10, gp0=11, gp1=12)
        order = ["qa", "ka", "va", "qb", "kb", "vb0", "vb1", "gb0", "gb1", "gp0", "bu0", "gp1", "bu1",
                 "ga0", "au", "ga1", "wo0", "wo1", "wq0", "wq1", "wq2", "wq3"]
        load_no = {n: k for k, n in enumerate(order)}

        def weight_source(name):
            if name in W_IN:
                return w_in[0, :, W_IN[name] * 512:(W_IN[name] + 1) * 512].rearrange("(c p) n -> p c n", p=P)
            if name == "au":
                return ins["w_a_up"][0].rearrange("(c p) n -> p c n", p=P)
            w = ins[{"bu": "w_b_up", "wo": "w_out", "wq": "peer_w_q"}[name[:2]]]
            k = int(name[2])
            return w[0, :, k * 512:(k + 1) * 512].rearrange("(c p) n -> p c n", p=P)

        w_landed = [sem(f"w_landed{k}") for k in range(W_BUFS)]
        last_use = {}
        next_load = [0]

        def load_weights(sp, upto):
            while next_load[0] < min(upto, len(order)):
                k = next_load[0]
                if k >= W_BUFS:
                    b, before = last_use[order[k - W_BUFS]]
                    sp.wait_ge(bank_full[b], before + 1)
                src = weight_source(order[k])
                c, n = src.shape[1], src.shape[2]
                dst = mem(W_AT + (k % W_BUFS) * W_SIZE, c, n)
                sp.dma_start(dst, src).then_inc(w_landed[k % W_BUFS], 16)
                next_load[0] += 1

        def weights_there(pe, name):
            k = load_no[name]
            pe.wait_ge(w_landed[k % W_BUFS], 16 * (k // W_BUFS + 1))
            return wbuf[k % W_BUFS]

        bank_full = [sem(f"bank_full{b}") for b in range(8)]
        bank_free = [sem(f"bank_free{b}") for b in range(8)]
        bank_uses = [0] * 8

        def take(b):
            bank_uses[b] += 1
            return b, bank_uses[b] - 1

        def pe_claims(pe, use):
            b, k = use
            if k:
                pe.wait_ge(bank_free[b], k)
            return ps[:, b, :]

        def filled(ins_, use):
            ins_.then_inc(bank_full[use[0]], 1)

        def reader_waits(eng, use):
            eng.wait_ge(bank_full[use[0]], use[1] + 1)
            return ps[:, use[0], :]

        def freed(ins_, use):
            ins_.then_inc(bank_free[use[0]], 1)

        def chained(eng, chain):
            def link(ins_):
                ins_.then_inc(chain[0], 1)
                chain[1] += 1
                eng.wait_ge(chain[0], chain[1])
            return link

        dve_chain = [sem("dve_chain"), 0]
        stored = sem("stored")
        n_stored = [0]

        def store(eng, dst, src):
            eng.dma_start(dst, src).then_inc(stored, 16)
            n_stored[0] += 1

        def transposes(pe, src, uses, ready, n_ready):
            for t in range(TILES):
                pe.wait_ge(ready, n_ready(t))
                for half in range(2):
                    bank = pe_claims(pe, uses[2 * t + half])
                    for c in range(4):
                        last = pe.transpose(bank[:, c * P:c * P + rows(t)],
                                            src(t)[0:rows(t), (half * 4 + c) * P:(half * 4 + c + 1) * P],
                                            ident[0:rows(t), 0:rows(t)])
                    filled(last, uses[2 * t + half])

        def transposed_to(dve, dst, uses, gain=None):
            for t in range(TILES):
                for half in range(2):
                    bank = reader_waits(dve, uses[2 * t + half])
                    src = bank.rearrange("p (c n) -> p c n", c=4)[:, :, 0:rows(t)]
                    out = dst[:, half * 4:half * 4 + 4, cols(t)]
                    if gain is None:
                        freed(dve.tensor_copy(out, src), uses[2 * t + half])
                    else:
                        g = gain[:, half * 4:half * 4 + 4].unsqueeze(2).to_broadcast([P, 4, rows(t)])
                        freed(dve.tensor_tensor(out, src, g, ALU.mult), uses[2 * t + half])

        consts_in, ident_in, small_in = sem("consts_in"), sem("ident_in"), sem("small_in")
        x_in = [sem(f"x_in{t}") for t in range(TILES)]
        assert CONST_AT["ident"][0] == 0 and CONST_AT["eps"][0] == CONST_N - 1
        sq0, root0, xn0 = sem("sq0"), sem("root0"), sem("xn0")
        X0 = mem(R, TILES, D)
        XN0 = mem(R + TILES * D, TILES, D)
        uses = [take(n % 8) for n in range(2 * TILES)]
        with nc.Block() as block:
            @block.sync
            def _(sp):
                sp.dma_start(X0[:, 0, :], ins["x_prompt"][0, cols(0), :]).then_inc(x_in[0], 16)
                with nc.allow_non_contiguous_dma(reason="small constants"):
                    for name in ("ident", "eps"):
                        at_, n_ = CONST_AT[name]
                        sp.dma_start(arena[:, at_:at_ + n_], consts[:, at_:at_ + n_]).then_inc(ident_in, 16)
                for t in range(1, PT):
                    sp.dma_start(X0[:, t, :], ins["x_prompt"][0, cols(t), :]).then_inc(x_in[t], 16)
                sp.dma_start(X0[0:NS, PT, :], ins["x_sample"].rearrange("b t d -> (b t) d")).then_inc(x_in[PT], 16)
                with nc.allow_non_contiguous_dma(reason="small parameters"):
                    sp.dma_start(mix_gain, ins["norm_mix_g"][0].rearrange("(c p) -> p c", p=P)).then_inc(small_in, 16)
                    sp.dma_start(ple_gain, ins["norm_ple_g"][0].rearrange("(c p) -> p c", p=P)).then_inc(small_in, 16)
                    sp.dma_start(qk_gain[:, 0, :], ins["q_norm_g"].to_broadcast([P, HD])).then_inc(small_in, 16)
                    sp.dma_start(qk_gain[:, 1, :], ins["k_norm_g"].to_broadcast([P, HD])).then_inc(small_in, 16)
                    sp.dma_start(bias_row, ins["sb_bias"].to_broadcast([P, H])).then_inc(small_in, 16)
                    for g in range(4):
                        sp.dma_start(bias_col[32 * g:32 * g + 32, :],
                                     ins["sb_bias"][0].rearrange("(h a b) -> h a b", a=1, b=1).to_broadcast([H, DECT, 1])
                                     ).then_inc(small_in, 16)
                sp.dma_start(table[:, :], ins["page_table"].rearrange("b n -> (b n)").rearrange("(a n) -> a n", a=1)).then_inc(small_in, 16)
                load_weights(sp, 1)
                sp.dma_start(arena[:, P:CONST_N - 1], consts[:, P:CONST_N - 1]).then_inc(consts_in, 16)
                load_weights(sp, W_BUFS)

            @block.scalar
            def _(act):
                act.wait_ge(ident_in, 32)
                for t in range(TILES):
                    r = rows(t)
                    act.wait_ge(x_in[t], 16)
                    act.activation(mem(HT_AT, D)[0:r, :], X0[0:r, t, :], ACT.Square,
                                   accum_out=stat[0:r, t:t + 1]).then_inc(sq0, 1)
                    act.wait_ge(sq0, t + 1)
                    act.activation(stat2[0:r, t:t + 1], stat[0:r, t:t + 1], ACT.Sqrt,
                                   bias=const("eps")[0:r, :], scale=1.0 / D).then_inc(root0, 1)

            @block.vector
            def _(dve):
                link = chained(dve, dve_chain)
                for t in range(TILES):
                    n = rows(t)
                    dve.wait_ge(root0, t + 1)
                    link(dve.reciprocal(stat[0:n, 8 + t:9 + t], stat2[0:n, t:t + 1]))
                    dve.tensor_scalar(XN0[0:n, t, :], X0[0:n, t, :], stat[0:n, 8 + t:9 + t], None,
                                      ALU.mult).then_inc(xn0, 1)
                dve.wait_ge(small_in, 16 * 10)
                dve.wait_ge(root0, TILES)
                transposed_to(dve, hT, uses, mix_gain)

            @block.tensor
            def _(pe):
                pe.wait_ge(ident_in, 32)
                transposes(pe, lambda t: XN0[:, t, :], uses, xn0, lambda t: t + 1)

        QT = mem(R + 10240, HP, SEQ)
        KT = mem(R + 12288, HP, SEQ)
        V = mem(R + 14336, PT, 512)
        SAMPLE_AT = R + 28000
        QTs = mem(SAMPLE_AT, HP, NS)
        KTs = mem(SAMPLE_AT + HP * NS, HP, NS)
        Vs = mem(SAMPLE_AT + 2 * HP * NS, 512)
        SQ = mem(R + 17152, 2, 512)
        QG = mem(R + 18176, 2, 512)
        QK = mem(R + 19200, 3, 512)
        s1_sq, s1_sum, s1_root, s1_tok = (sem("s1_" + n) for n in ("squares", "sums", "roots", "tokens"))
        kst = [sem(f"k_stored{n}") for n in range(3)]

        def project(pe, w, t, use, x=hT, nd=DC):
            bank = pe_claims(pe, use)
            for c in range(nd):
                last = pe.matmul(bank[0:rows(t), :], x[:, c, cols(t)], w[:, c, :],
                                 start=(c == 0), stop=(c == nd - 1))
            filled(last, use)

        def sample_parts(pe, w, use, x=hT, nd=DC):
            bank = pe_claims(pe, use)
            for c in range(nd):
                g = c % 4
                last = pe.matmul(bank[32 * g:32 * g + 32, :], x[:, c, SEQ:], w[:, c, :],
                                 start=(c < 4), stop=(c >= nd - 4), skip_group_check=True)
            filled(last, use)

        def keep_parts(act, parts, use, before=None):
            if before:
                act.wait_ge(bank_full[before[0]], before[1] + 1)
            bank = reader_waits(act, use)
            freed(act.activation(parts, bank, ACT.Copy), use)

        def sum_parts(pe, parts, part_use, use):
            pe.wait_ge(bank_free[part_use[0]], part_use[1] + 1)
            bank = pe_claims(pe, use)
            filled(pe.matmul(bank[0:NS, :], const("gather4"), parts, start=True, stop=True), use)

        groups = [(c, t) for c in range(3) for t in range(TILES)]
        proj = [take(n % 4) for n in range(len(groups))]
        part1 = [take(7) for _ in range(3)]
        PARTS1 = mem(R + 20736, 512)
        NQK = 2 * TILES
        last_use.update({order[c]: proj[n] for n, (c, t) in enumerate(groups)})
        turn = [take(4 + n % 3) for n in range(NQK)]
        with nc.Block() as block:
            @block.sync
            def _(sp):
                for n in range(NQK):
                    c, t = groups[n]
                    if c == 1:
                        sp.wait_ge(s1_tok, n + 1)
                        dst = outs["k_prompt"][0, 0, cols(t)] if t < PT else outs["k_sample"][0].rearrange("b t h d -> (b t) h d")
                        sp.dma_start(dst.rearrange("n h d -> n (h d)"), QK[0:rows(t), n % 3, :]).then_inc(kst[n % 3], 16)
                for t in range(TILES):
                    b, before = proj[NQK + t]
                    sp.wait_ge(bank_free[b], before + 1)
                    dst = outs["v_prompt"][0, 0, cols(t)] if t < PT else outs["v_sample"][0].rearrange("b t h d -> (b t) h d")
                    store(sp, dst.rearrange("n h d -> n (h d)"), V[:, t, :] if t < PT else Vs[0:NS, :])
                load_weights(sp, 6)
                sp.wait_ge(consts_in, 16)
                for k in range(3):
                    sp.wait_ge(kst[k], 16 * sum(1 for m in range(NQK) if groups[m][0] == 1 and m % 3 == k))

            @block.tensor
            def _(pe):
                def turn_back(n):
                    c, t = groups[n]
                    pe.wait_ge(s1_tok, n + 1)
                    bank = pe_claims(pe, turn[n])
                    for hp in range(HP):
                        last = pe.transpose(bank[:, hp * P:hp * P + rows(t)], QK[0:rows(t), n % 3, hp * P:(hp + 1) * P],
                                            ident[0:rows(t), 0:rows(t)])
                    filled(last, turn[n])
                for n, (c, t) in enumerate(groups):
                    w = weights_there(pe, order[c])
                    if t == 0:
                        sample_parts(pe, w, part1[c])
                    if t < PT:
                        project(pe, w, t, proj[n])
                    else:
                        if c == 0:
                            pe.wait_ge(consts_in, 16)
                        sum_parts(pe, PARTS1, part1[c], proj[n])
                    if 2 <= n < NQK + 2:
                        turn_back(n - 2)

            @block.scalar
            def _(act):
                def evacuate(n):
                    c, t = groups[n]
                    bank = reader_waits(act, turn[n])
                    full = (QT, KT)[c][:, :, cols(t)] if t < PT else (QTs, KTs)[c]
                    freed(act.activation(full, bank.rearrange("p (c n) -> p c n", c=4)[:, :, 0:rows(t)],
                                         ACT.Copy, scale=(HD ** -0.5 if c == 0 else 1.0)), turn[n])
                for n, (c, t) in enumerate(groups):
                    r = rows(t)
                    if t == 0:
                        keep_parts(act, PARTS1, part1[c], proj[n - 1] if n else None)
                    bank = reader_waits(act, proj[n])
                    if c < 2:
                        if n >= 2:
                            act.wait_ge(s1_sum, n - 1)
                        act.activation(SQ[0:r, n % 2, :], bank[0:r, :], ACT.Square).then_inc(s1_sq, 1)
                        act.wait_ge(s1_sum, n + 1)
                        act.activation(stat2[0:r, (n % 2) * 8:(n % 2) * 8 + 8], stat[0:r, (n % 2) * 8:(n % 2) * 8 + 8], ACT.Sqrt,
                                       bias=const("eps")[0:r, :], scale=1.0 / HD).then_inc(s1_root, 1)
                    else:
                        freed(act.activation(V[:, t, :] if t < PT else Vs[0:NS, :], bank[0:r, :], ACT.Copy), proj[n])
                    if 3 <= n < NQK + 3:
                        evacuate(n - 3)

            @block.vector
            def _(dve):
                link = chained(dve, dve_chain)
                for n in range(NQK):
                    c, t = groups[n]
                    r = rows(t)
                    so = (n % 2) * 8
                    dve.wait_ge(s1_sq, n + 1)
                    if n >= 2:
                        dve.wait_ge(s1_root, n - 1)
                    dve.tensor_reduce(stat[0:r, so:so + 8], SQ[0:r, n % 2, :].rearrange("p (h d) -> p h d", h=H), AX.X,
                                      ALU.add).then_inc(s1_sum, 1)
                    bank = reader_waits(dve, proj[n])
                    g = qk_gain[0:r, c:c + 1, :].to_broadcast([r, H, HD])
                    qg = QG[0:r, n % 2, :].rearrange("p (h d) -> p h d", h=H)
                    freed(dve.tensor_tensor(qg, bank[0:r, :].rearrange("p (h d) -> p h d", h=H), g, ALU.mult), proj[n])
                    dve.wait_ge(s1_root, n + 1)
                    link(dve.reciprocal(stat[0:r, 16 + so:24 + so], stat2[0:r, so:so + 8]))
                    dve.wait_ge(bank_free[proj[n][0]], proj[n][1] + 1)
                    if n >= 3:
                        dve.wait_ge(bank_full[turn[n - 3][0]], turn[n - 3][1] + 1)
                        if groups[n - 3][0] == 1:
                            dve.wait_ge(kst[n % 3], 16 * sum(1 for m in range(n - 2) if groups[m][0] == 1 and m % 3 == n % 3))
                    inv = stat[0:r, 16 + so:24 + so].unsqueeze(2).to_broadcast([r, H, HD])
                    dve.tensor_tensor(QK[0:r, n % 3, :].rearrange("p (h d) -> p h d", h=H), qg, inv, ALU.mult).then_inc(s1_tok, 1)

        KP = mem(R, 4, 4, 512)
        keys_in = [sem(f"keys_in{r}") for r in range(4)]
        values_in = [sem(f"values_in{r}") for r in range(4)]

        def page_ids(eng, b, half, r):
            return [eng.value_load(table[0:1, bass.ds(b * PAGES + half * 16 + 4 * g + r, 1)],
                                  min_val=0, max_val=ins["cache_k"].shape[1] - 1) for g in range(4)]

        def load_pages(eng, cache, ids, dst, landed):
            pages = ins[cache][0].rearrange("n p h d -> n p (h d)")
            for g in range(4):
                eng.dma_start(dst[:, g, :], pages[bass.ds(ids[g], 1)].rearrange("a p d -> p (a d)")).then_inc(landed, 16)

        WID = [(PT - j) * P for j in range(PT)]
        OFF = [sum(WID[:j]) for j in range(PT)]
        ZW = sum(WID)
        Z2 = mem(R + 17152, 2, ZW)
        E2 = mem(R + 19712, 2, ZW)
        SP2 = mem(R + 22272, 2, ZW)
        A2 = mem(R + 24832, 2, ZW)
        z_put, e_abs, e_exp, e_ln, sp_put, arg_put, a_put = (
            sem("pa_" + n) for n in ("z", "abs", "exp", "ln", "softplus", "arg", "weights"))
        score = {(h, j): take(j) for h in range(H) for j in range(PT)}
        suffix = {}
        for h in range(H):
            for j in range(PT - 1, -1, -1):
                suffix[h, j] = take(4 + len(suffix) % 3)
        attn_out = {h: take(7) for h in range(H)}
        with nc.Block() as block:
            @block.sync
            def _(sp):
                for r in range(4):
                    load_pages(sp, "cache_k", page_ids(sp, 0, 1, r), KP[:, r, :, :], keys_in[r])

            @block.tensor
            def _(pe):
                def scores(h):
                    lo = 64 * (h % 2)
                    for j in range(PT):
                        bank = pe_claims(pe, score[h, j])
                        filled(pe.matmul(bank[:, 0:WID[j]], KT[lo:lo + 64, h // 2, cols(j)],
                                         QT[lo:lo + 64, h // 2, j * P:], start=True, stop=True), score[h, j])

                def suffixes(h):
                    pe.wait_ge(sp_put, h + 1)
                    for j in range(PT - 1, -1, -1):
                        bank = pe_claims(pe, suffix[h, j])
                        last = pe.matmul(bank[:, 0:WID[j]], const("tri"), SP2[:, h % 2, OFF[j]:OFF[j] + WID[j]],
                                         start=True, stop=(j == PT - 1))
                        for k in range(j + 1, PT):
                            last = pe.matmul(bank[:, (k - j) * P:WID[j]], const("ones")[:, 0:P],
                                             SP2[:, h % 2, OFF[k]:OFF[k] + WID[k]], start=False, stop=(k == PT - 1))
                        filled(last, suffix[h, j])

                def outputs(h):
                    lo = 64 * (h % 2)
                    bank = pe_claims(pe, attn_out[h])
                    pe.wait_ge(a_put, h + 1)
                    for j in range(PT):
                        last = pe.matmul(bank[lo:lo + 64, j * P:], V[:, j, h * HD:(h + 1) * HD],
                                         A2[:, h % 2, OFF[j]:OFF[j] + WID[j]], start=(j == 0), stop=(j == PT - 1))
                    filled(last, attn_out[h])
                scores(0)
                for h in range(H):
                    if h + 1 < H:
                        scores(h + 1)
                    suffixes(h)
                    if h >= 1:
                        outputs(h - 1)
                outputs(H - 1)

            @block.vector
            def _(dve):
                link = chained(dve, dve_chain)

                def logits(h):
                    if h >= 2:
                        dve.wait_ge(arg_put, h - 1)
                    for j in range(PT):
                        bank = reader_waits(dve, score[h, j])
                        z = Z2[:, h % 2, OFF[j]:OFF[j] + WID[j]]
                        first = dve.scalar_tensor_tensor(out=z[:, 0:P], in0=bank[:, 0:P], scalar=bias_row[:, h:h + 1],
                                                         in1=const("diag_mask"), op0=ALU.add, op1=ALU.min)
                        if j < PT - 1:
                            link(first)
                            last = dve.tensor_scalar(z[:, P:], bank[:, P:WID[j]], bias_row[:, h:h + 1], None, ALU.add)
                        else:
                            last = first
                        freed(last, score[h, j])
                    for j in range(PT):
                        dve.wait_ge(bank_free[score[h, j][0]], score[h, j][1] + 1)
                    dve.sem_inc(z_put, 1)

                def softplus(h):
                    dve.wait_ge(e_ln, h + 1)
                    dve.scalar_tensor_tensor(out=SP2[:, h % 2, :], in0=Z2[:, h % 2, :], scalar=0.0, in1=E2[:, h % 2, :],
                                             op0=ALU.max, op1=ALU.add).then_inc(sp_put, 1)

                def arguments(h):
                    for j in range(PT - 1, -1, -1):
                        bank = reader_waits(dve, suffix[h, j])
                        z = Z2[:, h % 2, OFF[j]:OFF[j] + WID[j]]
                        freed(dve.tensor_tensor(z, z, bank[:, 0:WID[j]], ALU.subtract), suffix[h, j])
                    for j in range(PT):
                        dve.wait_ge(bank_free[suffix[h, j][0]], suffix[h, j][1] + 1)
                    dve.sem_inc(arg_put, 1)
                logits(0)
                for h in range(H):
                    softplus(h)
                    if h + 1 < H:
                        if h >= 1:
                            dve.wait_ge(a_put, h)
                        logits(h + 1)
                    arguments(h)

            @block.scalar
            def _(act):
                act.preload_act_table_set("natural_log_exp_and_others")

                def softplus_parts(h):
                    act.wait_ge(z_put, h + 1)
                    if h >= 2:
                        act.wait_ge(sp_put, h - 1)
                    e = E2[:, h % 2, :]
                    act.activation(e, Z2[:, h % 2, :], ACT.Abs).then_inc(e_abs, 1)
                    act.wait_ge(e_abs, h + 1)
                    act.activation(e, e, ACT.Exp, scale=-1.0).then_inc(e_exp, 1)
                    act.wait_ge(e_exp, h + 1)
                    act.activation(e, e, ACT.Ln, bias=1.0).then_inc(e_ln, 1)

                def weights(h):
                    act.wait_ge(arg_put, h + 1)
                    if h >= 2:
                        act.wait_ge(bank_full[7], attn_out[h - 2][1] + 1)
                    act.activation(A2[:, h % 2, :], Z2[:, h % 2, :], ACT.Exp).then_inc(a_put, 1)

                def keep(h):
                    lo = 64 * (h % 2)
                    bank = reader_waits(act, attn_out[h])
                    freed(act.activation(oaT[lo:lo + 64, h // 2, 0:SEQ], bank[lo:lo + 64, :], ACT.Copy), attn_out[h])
                softplus_parts(0)
                for h in range(H):
                    if h + 1 < H:
                        softplus_parts(h + 1)
                    weights(h)
                    if h >= 1:
                        keep(h - 1)
                keep(H - 1)

        VP = mem(R + 8192, 4, 4, 512)
        KPT = mem(R + 16384, 2, HP, 512)
        Zd, Ed, Cd, Ad = (mem(R + 20480 + 512 * n, 512) for n in range(4))
        AdT = mem(R + 22528, 4, P)
        Od = mem(R + 23040, 512)
        Qb = mem(R + 23552, HP, NS)
        Zn, En, Cn, An, AnT = (mem(R + 23680 + NS * n, NS) for n in range(5))
        tot = mem(R + 23840, 4)

        q_block, keys_turned, keys_kept, scores_done = (
            sem("d_" + n) for n in ("q_block", "keys_turned", "keys_kept", "scores_done"))
        zn_full, z_free, z_put, ln_put, sp_put, act_step = (
            sem("d_" + n) for n in ("zn_full", "z_free", "z_put", "ln_put", "softplus_put", "act_step"))
        scanned, new_total, total_put, carry_full, carry_put, arg_put = (
            sem("d_" + n) for n in ("scanned", "new_total", "total_put", "carry_full", "carry_put", "argument_put"))
        a_put, a_turned, a_kept, values_used = (
            sem("d_" + n) for n in ("weights_put", "weights_turned", "weights_kept", "values_used"))
        an_put, an_turned, an_kept, o_copied, o_turned, o_kept, q_zero = (
            sem("d_" + n) for n in ("new_weights_put", "new_weights_turned", "new_weights_kept", "o_copied",
                                    "o_turned", "o_kept", "q_zero"))

        with nc.Block() as block:
            @block.sync
            def _(sp):
                def load_keys(b, half):
                    for r in range(4):
                        ids = page_ids(sp, b, half, r)
                        sp.wait_ge(keys_turned, b * (8 * HP) + HP * (4 * (1 - half) + r + 1))
                        load_pages(sp, "cache_k", ids, KP[:, r, :, :], keys_in[r])

                with sp.Fori(0, DECB - 1) as b:
                    load_keys(b, 0)
                    load_keys(b + 1, 1)
                load_keys(DECB - 1, 0)

            @block.gpsimd
            def _(pool):
                def load_values(b, half):
                    for r in range(4):
                        ids = page_ids(pool, b, half, r)
                        pool.wait_ge(values_used, b * 2 + (2 - half))
                        load_pages(pool, "cache_v", ids, VP[:, r, :, :], values_in[r])
                pool.wait_ge(stored, 16 * n_stored[0])
                with pool.Fori(0, DECB) as b:
                    load_values(b, 1)
                    load_values(b, 0)

            @block.tensor
            def _(pe):
                pe.sem_inc(keys_turned, 4 * HP)
                pe.sem_inc(values_used, 1)

                def turn_keys(b, half, r):
                    n = 4 * (1 - half) + r
                    pe.wait_ge(keys_in[r], b * 128 + 64 * (2 - half))
                    for hp in range(HP):
                        pe.wait_ge(keys_kept, b * (8 * HP) + (HP * n + hp + 1))
                        for g in range(4):
                            last = pe.transpose(ps[:, hp, g * P:(g + 1) * P], KP[:, r, g, hp * P:(hp + 1) * P], ident)
                        last.then_inc(keys_turned, 1)

                def scores(b, half, r):
                    n = 4 * (1 - half) + r
                    pe.wait_ge(keys_kept, b * (8 * HP) + (HP * n + 2 * HP))
                    if r == 0:
                        pe.wait_ge(z_free, b * 2 + (2 - half))
                    for hp in range(HP):
                        for g in range(4):
                            last = pe.matmul(ps[32 * g:32 * g + 32, 4, r * P:(r + 1) * P], Qb[:, hp, :],
                                             KPT[:, r % 2, hp, g * P:(g + 1) * P], start=(hp == 0), stop=(hp == HP - 1),
                                             skip_group_check=True)
                    last.then_inc(scores_done, 1)

                def new_scores(b):
                    pe.wait_ge(q_block, b * 2 + 2)
                    for hp in range(HP):
                        last = pe.matmul(ps[0:NS, 6, 0:NS], Qb[:, hp, :], KTs[:, hp, :], start=(hp == 0), stop=(hp == HP - 1))
                    last.then_inc(zn_full, 1)

                def new_weights(b):
                    pe.wait_ge(an_put, b + 1)
                    pe.transpose(ps[0:NS, 6, P:2 * P], An, ident).then_inc(an_turned, 1)

                def carry(b, half):
                    m = 1 - half
                    pe.wait_ge(total_put, b * 2 + (m + 1))
                    pe.matmul(ps[:, 5, 64:65], const("spread")[0:NS, :], tot[0:NS, 2:3], start=True, stop=False)
                    if half == 0:
                        pe.matmul(ps[:, 5, 64:65], const("carry_all"), tot[:, 0:1], start=False, stop=False)
                    pe.matmul(ps[:, 5, 64:65], const("carry_in"), tot[:, m:m + 1], start=False,
                              stop=True).then_inc(carry_full, 1)

                def turn_weights(b, half, b2=None):
                    m = 1 - half
                    pe.wait_ge(a_put, b * 2 + (m + 2))
                    pe.wait_ge(a_kept, b * 2 + (m + 1))
                    if half == 1:
                        pe.wait_ge(an_kept, b + 1)
                    elif b2 is not None:
                        pe.wait_ge(z_put, b2 * 3 + 1)
                    for r in range(4):
                        last = pe.transpose(ps[:, 6, r * P:(r + 1) * P], Ad[:, r * P:(r + 1) * P], ident)
                    last.then_inc(a_turned, 1)

                def weigh_values(b, half):
                    m = 1 - half
                    if half == 1:
                        pe.wait_ge(o_copied, b + 1)
                        pe.wait_ge(an_kept, b + 1)
                        pe.matmul(ps[0:NS, 7, :], AnT, Vs, start=True, stop=False, skip_group_check=True)
                    pe.wait_ge(a_kept, b * 2 + (m + 2))
                    for r in range(4):
                        pe.wait_ge(values_in[r], b * 128 + 64 * (m + 1))
                        for g in range(4):
                            last = pe.matmul(ps[32 * g:32 * g + 32, 7, :], AdT[:, r, 32 * g:32 * g + 32], VP[:, r, g, :],
                                             start=(half == 1 and r == 0 and g > 0), stop=(half == 0 and r == 3),
                                             skip_group_check=True)
                    last.then_inc(values_used, 1)

                def turn_output(b):
                    pe.wait_ge(o_copied, b + 2)
                    pe.wait_ge(o_kept, b * 2 + 2)
                    for hp in range(HP):
                        last = pe.matmul(ps[:, 5, 256 + 8 * hp:264 + 8 * hp], Od[:, hp * P:(hp + 1) * P],
                                         const("select")[:, 8 * hp:8 * hp + 8], start=True, stop=True)
                    last.then_inc(o_turned, 1)

                def period(b, half, b2, half2):
                    turn_keys(b2, half2, 0)
                    turn_keys(b2, half2, 1)
                    if half2 == 1:
                        new_scores(b2)
                    else:
                        new_weights(b)
                    scores(b2, half2, 0)
                    carry(b, half)
                    turn_keys(b2, half2, 2)
                    scores(b2, half2, 1)
                    turn_weights(b, half, b2)
                    turn_keys(b2, half2, 3)
                    scores(b2, half2, 2)
                    weigh_values(b, half)
                    scores(b2, half2, 3)
                    if half == 0:
                        turn_output(b)
                new_scores(0)
                turn_keys(0, 1, 0)
                for r in range(4):
                    if r < 3:
                        turn_keys(0, 1, r + 1)
                    scores(0, 1, r)
                with pe.Fori(0, DECB - 1) as b:
                    period(b, 1, b, 0)
                    period(b, 0, b + 1, 1)
                period(DECB - 1, 1, DECB - 1, 0)
                carry(DECB - 1, 0)
                turn_weights(DECB - 1, 0)
                weigh_values(DECB - 1, 0)
                turn_output(DECB - 1)

            @block.scalar
            def _(act):
                act.preload_act_table_set("natural_log_exp_and_others")
                act.wait_ge(q_zero, 10)
                act.sem_inc(a_kept, 1)
                act.sem_inc(keys_kept, HP)
                act.sem_inc(o_copied, 1)
                act.sem_inc(a_put, 1)

                def keep_keys(b, half, r):
                    n = 4 * (1 - half) + r
                    act.wait_ge(scores_done, b * 8 + (n + 1))
                    for hp in range(HP):
                        act.wait_ge(keys_turned, b * (8 * HP) + (HP * n + hp + 1 + 4 * HP))
                        act.activation(KPT[:, r % 2, hp, :], ps[:, hp, :], ACT.Copy).then_inc(keys_kept, 1)

                def softplus_parts(z, e, b, k):
                    act.wait_ge(z_put, b * 3 + (k + 1))
                    act.activation(e, z, ACT.Abs).then_inc(act_step, 1)
                    act.wait_ge(act_step, b * 6 + (2 * k + 1))
                    act.activation(e, e, ACT.Exp, scale=-1.0).then_inc(act_step, 1)
                    act.wait_ge(act_step, b * 6 + (2 * k + 2))
                    act.activation(e, e, ACT.Ln, bias=1.0).then_inc(ln_put, 1)

                def new_weights(b):
                    act.wait_ge(arg_put, b * 3 + 1)
                    act.activation(An[0:NS, :], Cn[0:NS, :], ACT.Exp).then_inc(an_put, 1)

                def weights(b, half):
                    m = 1 - half
                    act.wait_ge(arg_put, b * 3 + (2 + m))
                    act.activation(Ad, Cd, ACT.Exp).then_inc(a_put, 1)
                    act.wait_ge(a_turned, b * 2 + (m + 1))
                    act.wait_ge(values_used, b * 2 + (m + 1))
                    act.activation(AdT.rearrange("p r n -> p (r n)"), ps[:, 6, :], ACT.Copy).then_inc(a_kept, 1)

                def copy_output(b):
                    act.wait_ge(values_used, b * 2 + 3)
                    act.activation(Od, ps[:, 7, :], ACT.Copy).then_inc(o_copied, 1)

                def period(b, half, b2, half2):
                    keep_keys(b2, half2, 0)
                    softplus_parts(Zd, Ed, b, 2 - half)
                    keep_keys(b2, half2, 1)
                    if half2 == 0:
                        act.wait_ge(an_turned, b + 1)
                        act.activation(AnT[0:NS, :], ps[0:NS, 6, P:P + NS], ACT.Copy).then_inc(an_kept, 1)
                    keep_keys(b2, half2, 2)
                    weights(b, half)
                    if half2 == 1:
                        softplus_parts(Zn[0:NS, :], En[0:NS, :], b2, 0)
                    keep_keys(b2, half2, 3)
                    if half2 == 1:
                        new_weights(b2)
                        copy_output(b)
                softplus_parts(Zn[0:NS, :], En[0:NS, :], 0, 0)
                for r in range(4):
                    keep_keys(0, 1, r)
                new_weights(0)
                with act.Fori(0, DECB - 1) as b:
                    period(b, 1, b, 0)
                    period(b, 0, b + 1, 1)
                period(DECB - 1, 1, DECB - 1, 0)
                softplus_parts(Zd, Ed, DECB - 1, 2)
                weights(DECB - 1, 0)
                copy_output(DECB - 1)

            @block.vector
            def _(dve):
                qb_flat = Qb.rearrange("p a b -> p (a b)")
                dve.memset(qb_flat, 0.0).then_inc(q_zero, 1)
                for g in range(1, 4):
                    for buf in (An, AnT, Vs):
                        dve.memset(buf[32 * g:32 * g + 32, :], 0.0).then_inc(q_zero, 1)
                dve.wait_ge(q_zero, 10)
                dve.sem_inc(z_free, 1)
                dve.sem_inc(o_kept, 2)
                dve.sem_inc(scores_done, 2)

                def queries(b):
                    for j in range(2):
                        own = qb_flat[64 * j:64 * j + 64, DECT * j:DECT * j + 1]
                        dst = bass.AP(own.tensor, own.offset, [list(own.ap[0]), [NS + 2 * DECT, HP], [1, DECT]])
                        dve.tensor_copy(dst, QTs[64 * j:64 * j + 64, :, bass.ds(b * DECT, DECT)]).then_inc(q_block, 1)

                def new_keys(b):
                    dve.wait_ge(zn_full, b + 1)
                    dve.scalar_tensor_tensor(out=Zn[0:NS, :], in0=ps[0:NS, 6, 0:NS], scalar=bias_col[0:NS, :],
                                             in1=const("new_mask")[0:NS, bass.ds(b * NS, NS)], op0=ALU.add,
                                             op1=ALU.min).then_inc(z_put, 1)
                    dve.wait_ge(ln_put, b * 3 + 1)
                    dve.scalar_tensor_tensor(out=En[0:NS, :], in0=Zn[0:NS, :], scalar=0.0, in1=En[0:NS, :],
                                             op0=ALU.max, op1=ALU.add).then_inc(sp_put, 1)
                    dve.wait_ge(sp_put, b * 3 + 1)
                    dve.tensor_tensor_scan(Cn[0:NS, ::-1], const("ones")[0:NS, 0:NS], En[0:NS, ::-1], 0.0,
                                           ALU.mult, ALU.add).then_inc(scanned, 1)
                    dve.wait_ge(scanned, b * 3 + 1)
                    dve.tensor_copy(tot[0:NS, 2:3], Cn[0:NS, 0:1]).then_inc(new_total, 1)
                    dve.wait_ge(new_total, b + 1)
                    dve.tensor_tensor(Cn[0:NS, :], Zn[0:NS, :], Cn[0:NS, :], ALU.subtract).then_inc(arg_put, 1)

                def logits(b, half):
                    m = 1 - half
                    dve.wait_ge(scores_done, b * 8 + (4 * m + 6))
                    dve.tensor_scalar(Zd, ps[:, 4, :], bias_col, None, ALU.add).then_inc(z_put, 1)
                    dve.wait_ge(z_put, b * 3 + (2 + m))
                    dve.sem_inc(z_free, 1)

                def sums(b, half):
                    m = 1 - half
                    dve.wait_ge(ln_put, b * 3 + (2 + m))
                    dve.scalar_tensor_tensor(out=Ed, in0=Zd, scalar=0.0, in1=Ed, op0=ALU.max,
                                             op1=ALU.add).then_inc(sp_put, 1)
                    dve.wait_ge(sp_put, b * 3 + (2 + m))
                    dve.wait_ge(a_put, b * 2 + (m + 1))
                    dve.tensor_tensor_scan(Cd[:, ::-1], const("ones"), Ed[:, ::-1], 0.0, ALU.mult,
                                           ALU.add).then_inc(scanned, 1)
                    dve.wait_ge(scanned, b * 3 + (2 + m))
                    dve.tensor_copy(tot[:, m:m + 1], Cd[:, 0:1]).then_inc(total_put, 1)
                    dve.wait_ge(carry_full, b * 2 + (m + 1))
                    dve.tensor_copy(tot[:, 3:4], ps[:, 5, 64:65]).then_inc(carry_put, 1)
                    dve.wait_ge(carry_put, b * 2 + (m + 1))
                    dve.scalar_tensor_tensor(out=Cd, in0=Zd, scalar=tot[:, 3:4], in1=Cd, op0=ALU.subtract,
                                             op1=ALU.subtract).then_inc(arg_put, 1)

                def output(b):
                    dve.wait_ge(o_turned, b + 1)
                    for j in range(2):
                        src = ps[64 * j:64 * j + 64, 5, 256:288].rearrange("p (a j t) -> p a j t", a=HP, j=2)[:, :, j, :]
                        dve.tensor_copy(oaT[64 * j:64 * j + 64, :, bass.ds(b * DECT + SEQ, DECT)], src).then_inc(o_kept, 1)
                queries(0)
                new_keys(0)
                with dve.Fori(0, DECB - 1) as b:
                    logits(b, 1)
                    sums(b, 1)
                    logits(b, 0)
                    queries(b + 1)
                    sums(b, 0)
                    new_keys(b + 1)
                    output(b)
                logits(DECB - 1, 1)
                sums(DECB - 1, 1)
                logits(DECB - 1, 0)
                sums(DECB - 1, 0)
                output(DECB - 1)

        QBT = mem(R, RH, TOK)
        KBT = mem(R + 2176, RH, TOK)
        KB = mem(R + 4352, TILES, 512)
        VB = mem(R + 6912, TILES, D)
        RAW = mem(R + 17152, 2, 512)
        RC = mem(R + 18176, 2, 512)
        RS = mem(R + 19200, 2, 512)
        QR = mem(R + 20224, 3, 512)
        cos_put, sin_put, rot_put = (sem("rope_" + n) for n in ("cos", "sin", "out"))
        groups_rope = [(c, t) for c in range(4) for t in range(TILES)]
        proj4 = [take(n % 4) for n in range(len(groups_rope))]
        turn4 = [take(4 + n % 3) for n in range(NQK)]
        part4 = [take(7) for _ in range(4)]
        PARTS4 = mem(R + 22016, 512)
        names = ["qb", "kb", "vb0", "vb1"]
        last_use.update({names[c]: proj4[n] for n, (c, t) in enumerate(groups_rope)})

        def rotated(n):
            c, t = groups_rope[n]
            return QR[:, n % 3, :] if c == 0 else KB[:, t, :]
        with nc.Block() as block:
            @block.sync
            def _(sp):
                load_weights(sp, load_no["vb1"] + 4)

            @block.tensor
            def _(pe):
                def turn_back(n):
                    c, t = groups_rope[n]
                    pe.wait_ge(rot_put, n + 1)
                    bank = pe_claims(pe, turn4[n])
                    for h in range(RH):
                        last = pe.transpose(bank[:, h * P:h * P + rows(t)], rotated(n)[0:rows(t), h * P:(h + 1) * P],
                                            ident[0:rows(t), 0:rows(t)])
                    filled(last, turn4[n])
                for n, (c, t) in enumerate(groups_rope):
                    w = weights_there(pe, names[c])
                    if t == 0:
                        sample_parts(pe, w, part4[c])
                    if t < PT:
                        project(pe, w, t, proj4[n])
                    else:
                        sum_parts(pe, PARTS4, part4[c], proj4[n])
                    if 2 <= n < NQK + 2:
                        turn_back(n - 2)

            @block.scalar
            def _(act):
                def evacuate(n):
                    c, t = groups_rope[n]
                    bank = reader_waits(act, turn4[n])
                    freed(act.activation((QBT, KBT)[c][:, :, cols(t)],
                                         bank.rearrange("p (c n) -> p c n", c=4)[:, :, 0:rows(t)], ACT.Copy), turn4[n])
                for n, (c, t) in enumerate(groups_rope):
                    r = rows(t)
                    if t == 0:
                        keep_parts(act, PARTS4, part4[c], proj4[n - 1] if n else None)
                    bank = reader_waits(act, proj4[n])
                    if c < 2:
                        if n >= 2:
                            act.wait_ge(sin_put, n - 1)
                        freed(act.activation(RAW[0:r, n % 2, :], bank[0:r, :], ACT.Copy,
                                             scale=(1.0 if c == 0 else RK ** -0.5)), proj4[n])
                    else:
                        freed(act.activation(VB[0:r, t, (c - 2) * 512:(c - 1) * 512], bank[0:r, :], ACT.Copy), proj4[n])
                    if 3 <= n < NQK + 3:
                        evacuate(n - 3)

            @block.vector
            def _(dve):
                for n in range(NQK):
                    c, t = groups_rope[n]
                    r = rows(t)
                    b, before = proj4[n]
                    dve.wait_ge(bank_free[b], before + 1)
                    raw = RAW[0:r, n % 2, :].rearrange("p (h a d) -> p h a d", h=RH, a=2)
                    pc = RC[0:r, n % 2, :].rearrange("p (a d) -> p a d", a=2 * RH)
                    pr = RS[0:r, n % 2, :].rearrange("p (h a d) -> p h a d", h=RH, a=2)
                    cosr = const("cos", TILES, 64)[0:r, t:t + 1, :].to_broadcast([r, 2 * RH, 64])
                    sinr = const("sin", TILES, 2, 64)[0:r, t:t + 1, :, :].to_broadcast([r, RH, 2, 64])
                    dve.tensor_tensor(pc, RAW[0:r, n % 2, :].rearrange("p (a d) -> p a d", a=2 * RH), cosr, ALU.mult).then_inc(cos_put, 1)
                    dve.tensor_tensor(pr, raw[:, :, ::-1, :], sinr, ALU.mult).then_inc(sin_put, 1)
                    dve.wait_ge(cos_put, n + 1)
                    dve.wait_ge(sin_put, n + 1)
                    if 3 <= n < TILES + 3:
                        b, before = turn4[n - 3]
                        dve.wait_ge(bank_full[b], before + 1)
                    dve.tensor_tensor(rotated(n)[0:r, :], RC[0:r, n % 2, :], RS[0:r, n % 2, :], ALU.add).then_inc(rot_put, 1)

        import math
        OB = mem(R + 12032, TILES, D)
        SD = mem(R + 17152, 2, P)
        QS = mem(R + 17408, 2, P)
        KD = mem(R + 17664, 2, P)
        ST = mem(R + 17920, RH, RV)
        SB = mem(R + 18944, 2, RH, RV)
        SO = mem(R + 20992, 2, RH, RV)
        QSs = mem(R + 23040, RH, NS)
        QM = mem(R + 23168, RH, DECB, NS)
        KM = mem(R + 24192, 2, RH, P)
        SDs = mem(R + 25216, RH, NS)
        JUNK = mem(R + 25344, 2, RV)
        gain_ret = mem(R + 25856, D)
        gamma_p = [math.exp(P * g) for g in gammas()]
        gamma_s = [math.exp(DECT * g) for g in gammas()]
        work = [(c, h) for c in range(PT) for h in range(RH)]
        NW = len(work)
        sc_use = [take(m % 2) for m in range(NW)]
        ob_use = [take(2 + m % 2) for m in range(NW)]
        st_use = [take(4 + m % 2) for m in range(NW)]
        s_sc = take(6)
        s_ob = take(2)
        s_st = [[take(4 + 2 * (b % 2)), take(5 + 2 * (b % 2))] for b in range(DECB)]
        sd_put, qs_put, kd_put, st_put, ob_sq, gain_in = (
            sem("ret_" + n) for n in ("scores_decayed", "q_decayed", "k_decayed", "state", "squares", "gain"))
        qss_put, qm_put, km_put, sds_put, so_put = (sem("rets_" + n) for n in ("q", "q_masked", "k_masked", "scores", "state"))
        sb_in = [sem(f"state_in{k}") for k in range(2)]
        so_out = [sem(f"state_out{k}") for k in range(2)]
        ob_put = sem("ob_put")
        with nc.Block() as block:
            @block.sync
            def _(sp):
                sp.dma_start(gain_ret, ins["ret_norm_g"][0].rearrange("(a h) d -> a (h d)", a=1).to_broadcast([P, D])).then_inc(gain_in, 16)
                for b in range(2):
                    sp.dma_start(SB[:, b, :, :], ins["state_ret"][0, b].rearrange("h d e -> d h e")).then_inc(sb_in[b], 16)
                sp.wait_ge(st_put, NW)
                store(sp, outs["ret_prompt"][0, 0].rearrange("h d e -> d h e"), ST)
                for b in range(DECB):
                    sp.wait_ge(so_put, RH * (b + 1))
                    sp.dma_start(outs["ret_sample"][0, b].rearrange("h d e -> d h e"), SO[:, b % 2, :, :]).then_inc(so_out[b % 2], 16)
                    if b + 2 < DECB:
                        sp.dma_start(SB[:, b % 2, :, :], ins["state_ret"][0, b + 2].rearrange("h d e -> d h e")).then_inc(sb_in[b % 2], 16)
                load_weights(sp, load_no["vb1"] + 4)
                sp.wait_ge(stored, 16 * n_stored[0])
                for k in range(2):
                    sp.wait_ge(so_out[k], 16 * (DECB // 2))

            @block.tensor
            def _(pe):
                def outputs(m):
                    c, h = work[m]
                    pe.wait_ge(sd_put, m + 1)
                    bank = pe_claims(pe, ob_use[m])
                    last = pe.matmul(bank[:, 0:RV], SD[:, m % 2, :], VB[:, c, h * RV:(h + 1) * RV], start=True, stop=(c == 0))
                    if c:
                        pe.wait_ge(st_put, m - RH + 1)
                        pe.wait_ge(qs_put, m + 1)
                        last = pe.matmul(bank[:, 0:RV], QS[:, m % 2, :], ST[:, h, :], start=False, stop=True)
                    filled(last, ob_use[m])
                    bank = pe_claims(pe, st_use[m])
                    pe.wait_ge(kd_put, m + 1)
                    filled(pe.matmul(bank[:, 0:RV], KD[:, m % 2, :], VB[:, c, h * RV:(h + 1) * RV], start=True, stop=True), st_use[m])
                for m, (c, h) in enumerate(work):
                    bank = pe_claims(pe, sc_use[m])
                    filled(pe.matmul(bank[:, 0:P], KBT[:, h, cols(c)], QBT[:, h, cols(c)], start=True, stop=True), sc_use[m])
                    if m:
                        outputs(m - 1)
                outputs(NW - 1)
                bank = pe_claims(pe, s_sc)
                for h in range(RH):
                    last = pe.matmul(bank[0:NS, h * NS:(h + 1) * NS], KBT[:, h, SEQ:], QBT[:, h, SEQ:], start=True, stop=True)
                filled(last, s_sc)
                pe.wait_ge(sds_put, 1)
                out = pe_claims(pe, s_ob)
                for h in range(RH):
                    pe.matmul(out[NS * h:NS * (h + 1), 0:RV], SDs[0:NS, h, :], VB[0:NS, PT, h * RV:(h + 1) * RV],
                              start=True, stop=False, skip_group_check=True)
                pe.wait_ge(qm_put, RH)
                for b in range(DECB):
                    pe.wait_ge(sb_in[b % 2], 16 * (b // 2 + 1))
                    for h in range(RH):
                        last = pe.matmul(out[NS * h:NS * (h + 1), 0:RV], QM[:, h, b, :], SB[:, b % 2, h, :],
                                         start=False, stop=(b == DECB - 1), skip_group_check=True)
                    if b == DECB - 1:
                        filled(last, s_ob)
                    pe.wait_ge(km_put, b + 1)
                    for k in range(2):
                        bank = pe_claims(pe, s_st[b][k])
                        for h in (2 * k, 2 * k + 1):
                            last = pe.matmul(bank[:, (h % 2) * RV:(h % 2 + 1) * RV], KM[0:NS, b % 2, h, :],
                                             VB[0:NS, PT, h * RV:(h + 1) * RV], start=True, stop=True)
                        filled(last, s_st[b][k])

            @block.scalar
            def _(act):
                for m, (c, h) in enumerate(work):
                    bank = reader_waits(act, ob_use[m])
                    if m >= 2:
                        act.wait_ge(ob_sq, m - 1)
                    act.activation(JUNK[:, m % 2, :], bank[:, 0:RV], ACT.Square, accum_out=stat[:, m:m + 1]).then_inc(ob_sq, 1)
                    freed(act.activation(OB[:, c, h * RV:(h + 1) * RV], bank[:, 0:RV], ACT.Copy), ob_use[m])
                for h in range(RH):
                    bank = reader_waits(act, s_ob)
                    m = NW + h
                    act.wait_ge(ob_sq, m - 1)
                    src = bank[NS * h:NS * (h + 1), 0:RV]
                    act.activation(JUNK[0:NS, m % 2, :], src, ACT.Square, accum_out=stat[0:NS, m:m + 1]).then_inc(ob_sq, 1)
                    last = act.activation(OB[0:NS, PT, h * RV:(h + 1) * RV], src, ACT.Copy)
                    if h == RH - 1:
                        freed(last, s_ob)
                act.wait_ge(ob_sq, NW + RH)
                act.activation(stat2[:, 0:NW], stat[:, 0:NW], ACT.Sqrt, bias=const("eps"), scale=1.0 / RV).then_inc(ob_put, 1)
                act.activation(stat2[0:NS, NW:NW + RH], stat[0:NS, NW:NW + RH], ACT.Sqrt, bias=const("eps")[0:NS, :],
                               scale=1.0 / RV).then_inc(ob_put, 1)

            @block.vector
            def _(dve):
                def state(m):
                    c, h = work[m]
                    bank = reader_waits(dve, st_use[m])
                    dve.wait_ge(bank_full[ob_use[m][0]], ob_use[m][1] + 1)
                    if c == 0:
                        ins_ = dve.tensor_copy(ST[:, h, :], bank[:, 0:RV])
                    else:
                        ins_ = dve.scalar_tensor_tensor(out=ST[:, h, :], in0=ST[:, h, :], scalar=gamma_p[h], in1=bank[:, 0:RV],
                                                        op0=ALU.mult, op1=ALU.add)
                    freed(ins_, st_use[m])
                    dve.wait_ge(bank_free[st_use[m][0]], st_use[m][1] + 1)
                    dve.sem_inc(st_put, 1)
                for m, (c, h) in enumerate(work):
                    bank = reader_waits(dve, sc_use[m])
                    if m >= 2:
                        dve.wait_ge(bank_full[ob_use[m - 2][0]], ob_use[m - 2][1] + 1)
                    ins_ = dve.tensor_tensor(SD[:, m % 2, :], bank[:, 0:P], const("decay", RH, P)[:, h, :], ALU.mult)
                    freed(ins_, sc_use[m])
                    dve.wait_ge(bank_free[sc_use[m][0]], sc_use[m][1] + 1)
                    dve.sem_inc(sd_put, 1)
                    if m:
                        state(m - 1)
                state(NW - 1)
                bank = reader_waits(dve, s_sc)
                dve.tensor_tensor(SDs[0:NS], bank[0:NS, 0:RH * NS].rearrange("p (h n) -> p h n", h=RH),
                                  const("s_decay", RH, NS)[0:NS], ALU.mult).then_inc(sds_put, 1)
                dve.wait_ge(sds_put, 1)
                dve.sem_inc(bank_free[s_sc[0]], 1)
                for b in range(DECB):
                    if b >= 2:
                        dve.wait_ge(so_out[b % 2], 16 * (b // 2))
                    for h in range(RH):
                        bank = reader_waits(dve, s_st[b][h // 2])
                        dve.scalar_tensor_tensor(out=SO[:, b % 2, h, :], in0=SB[:, b % 2, h, :], scalar=gamma_s[h],
                                                 in1=bank[:, (h % 2) * RV:(h % 2 + 1) * RV], op0=ALU.mult,
                                                 op1=ALU.add).then_inc(so_put, 1)
                        if h % 2:
                            dve.wait_ge(so_put, RH * b + h + 1)
                            dve.sem_inc(bank_free[s_st[b][h // 2][0]], 1)

            @block.gpsimd
            def _(pool):
                for m, (c, h) in enumerate(work):
                    if m >= 2:
                        pool.wait_ge(bank_full[st_use[m - 2][0]], st_use[m - 2][1] + 1)
                    pool.tensor_tensor(QS[:, m % 2, :], QBT[:, h, cols(c)], const("q_decay", RH, P)[:, h, :], ALU.mult).then_inc(qs_put, 1)
                    pool.tensor_tensor(KD[:, m % 2, :], KB[:, c, h * P:(h + 1) * P],
                                       const("k_decay")[:, h:h + 1].to_broadcast([P, P]), ALU.mult).then_inc(kd_put, 1)
                pool.tensor_tensor(QSs, QBT[:, :, SEQ:], const("s_q_decay", RH, NS), ALU.mult).then_inc(qss_put, 1)
                pool.wait_ge(qss_put, 1)
                for h in range(RH):
                    pool.tensor_tensor(QM[:, h, :, :], QSs[:, h:h + 1, :].to_broadcast([P, DECB, NS]),
                                       const("s_block", DECB, NS), ALU.mult).then_inc(qm_put, 1)
                for b in range(DECB):
                    if b >= 2:
                        u = s_st[b - 2][1]
                        pool.wait_ge(bank_full[u[0]], u[1] + 1)
                    pool.tensor_tensor(KM[0:NS, b % 2], KB[0:NS, PT, :].rearrange("p (h d) -> p h d", h=RH),
                                       const("s_k_decay", DECB, RH)[0:NS, b, :].unsqueeze(2).to_broadcast([NS, RH, P]),
                                       ALU.mult).then_inc(km_put, 1)

        OBT = mem(R, DC, TOK)
        GATE = mem(R + 17152, 2, 512)
        groups6 = [(c, t) for c in range(2) for t in range(TILES)]
        proj6 = [take(n % 4) for n in range(len(groups6))]
        turn6 = [take(4 + n % 3) for n in range(len(groups6))]
        part6 = [take(7) for _ in range(2)]
        PARTS6 = mem(R + 20480, 512)
        last_use.update({f"gb{c}": proj6[n] for n, (c, t) in enumerate(groups6)})
        ob_ready, ob_half = sem("ob_gated"), sem("ob_normed")
        inv_put = sem("ob_inverse")
        with nc.Block() as block:
            @block.sync
            def _(sp):
                load_weights(sp, load_no["gb1"] + 4)

            @block.tensor
            def _(pe):
                def turn_back(n):
                    c, t = groups6[n]
                    pe.wait_ge(ob_ready, n + 1)
                    bank = pe_claims(pe, turn6[n])
                    for k in range(4):
                        last = pe.transpose(bank[:, k * P:k * P + rows(t)], OB[0:rows(t), t, (4 * c + k) * P:(4 * c + k + 1) * P],
                                            ident[0:rows(t), 0:rows(t)])
                    filled(last, turn6[n])
                for n, (c, t) in enumerate(groups6):
                    w = weights_there(pe, f"gb{c}")
                    if t == 0:
                        sample_parts(pe, w, part6[c])
                    if t < PT:
                        project(pe, w, t, proj6[n])
                    else:
                        sum_parts(pe, PARTS6, part6[c], proj6[n])
                    if n >= 2:
                        turn_back(n - 2)
                for n in range(len(groups6) - 2, len(groups6)):
                    turn_back(n)

            @block.scalar
            def _(act):
                def evacuate(n):
                    c, t = groups6[n]
                    bank = reader_waits(act, turn6[n])
                    freed(act.activation(OBT[:, 4 * c:4 * c + 4, cols(t)],
                                         bank.rearrange("p (c n) -> p c n", c=4)[:, :, 0:rows(t)], ACT.Copy), turn6[n])
                for n, (c, t) in enumerate(groups6):
                    if t == 0:
                        keep_parts(act, PARTS6, part6[c], proj6[n - 1] if n else None)
                    bank = reader_waits(act, proj6[n])
                    if n >= 2:
                        act.wait_ge(ob_ready, n - 1)
                    freed(act.activation(GATE[0:rows(t), n % 2, :], bank[0:rows(t), :], ACT.Silu), proj6[n])
                    if n >= 3:
                        evacuate(n - 3)
                for n in range(len(groups6) - 3, len(groups6)):
                    evacuate(n)

            @block.vector
            def _(dve):
                dve.wait_ge(ob_put, 2)
                dve.wait_ge(gain_in, 16)
                dve.reciprocal(stat[:, 0:NW], stat2[:, 0:NW]).then_inc(inv_put, 1)
                dve.reciprocal(stat[0:NS, NW:NW + RH], stat2[0:NS, NW:NW + RH]).then_inc(inv_put, 1)
                dve.wait_ge(inv_put, 2)
                for n, (c, t) in enumerate(groups6):
                    r = rows(t)
                    for k in range(2):
                        h = 2 * c + k
                        o = OB[0:r, t, h * RV:(h + 1) * RV]
                        dve.scalar_tensor_tensor(out=o, in0=o, scalar=stat[0:r, 4 * t + h:4 * t + h + 1],
                                                 in1=gain_ret[0:r, h * RV:(h + 1) * RV], op0=ALU.mult, op1=ALU.mult).then_inc(ob_half, 1)
                    dve.wait_ge(ob_half, 2 * n + 2)
                    b, before = proj6[n]
                    dve.wait_ge(bank_free[b], before + 1)
                    o = OB[0:r, t, c * 512:(c + 1) * 512]
                    dve.tensor_tensor(o, o, GATE[0:r, n % 2, :], ALU.mult).then_inc(ob_ready, 1)

        SG = mem(R + 4352, TILES, 512)
        M = mem(R + 17152, TILES, D)
        MTMP = mem(R + 22272, 2, 512)
        seq = [("gp0", 0), ("bu0", 0), ("gp1", 1), ("bu1", 1), ("ga0", 0), ("au", 0), ("ga1", 1), ("au", 1)]
        proj7 = {(k, t): take(4 * (k % 2) + (TILES * (k // 2) + t) % (4 - k % 2)) for k in range(len(seq)) for t in range(TILES)}
        part7 = [take(7) for _ in seq]
        PARTS7 = mem(R + 23296, 512)
        for k, (name, _) in enumerate(seq):
            last_use[name] = proj7[k, PT]
        product, merged = sem("merge_product"), sem("merged")
        with nc.Block() as block:
            @block.sync
            def _(sp):
                load_weights(sp, load_no["ga1"] + 4)

            @block.tensor
            def _(pe):
                for k, (name, n) in enumerate(seq):
                    w, x, nd = weights_there(pe, name), OBT if name[0:2] == "bu" else hT, DC
                    if name == "au":
                        w = w.rearrange("p a b -> p (a b)").rearrange("p (c n) -> p c n", c=HP)[:, :, n * 512:(n + 1) * 512]
                        x, nd = oaT, HP
                    sample_parts(pe, w, part7[k], x, nd)
                    for t in range(PT):
                        project(pe, w, t, proj7[k, t], x, nd)
                    sum_parts(pe, PARTS7, part7[k], proj7[k, PT])

            @block.scalar
            def _(act):
                for k in range(len(seq)):
                    keep_parts(act, PARTS7, part7[k], proj7[k - 1, PT] if k else None)
                    if k % 2:
                        continue
                    for t in range(TILES):
                        bank = reader_waits(act, proj7[k, t])
                        if k:
                            act.wait_ge(product, TILES * (k // 2 - 1) + t + 1)
                        freed(act.activation(SG[0:rows(t), t, :], bank[0:rows(t), :], ACT.Sigmoid), proj7[k, t])

            @block.vector
            def _(dve):
                for k in range(1, len(seq), 2):
                    n = seq[k][1]
                    for t in range(TILES):
                        r = rows(t)
                        m = TILES * (k // 2) + t
                        bank = reader_waits(dve, proj7[k, t])
                        b, before = proj7[k - 1, t]
                        dve.wait_ge(bank_free[b], before + 1)
                        dst = M[0:r, t, n * 512:(n + 1) * 512]
                        if k < 4:
                            ins_ = dve.tensor_tensor(dst, bank[0:r, :], SG[0:r, t, :], ALU.mult)
                        else:
                            if m >= 2 * TILES + 2:
                                dve.wait_ge(merged, m - 2 * TILES - 1)
                            ins_ = dve.tensor_tensor(MTMP[0:r, m % 2, :], bank[0:r, :], SG[0:r, t, :], ALU.mult)
                        ins_.then_inc(product, 1)
                        dve.wait_ge(product, m + 1)
                        dve.sem_inc(bank_free[proj7[k, t][0]], 1)
                        if k > 4:
                            dve.tensor_tensor(dst, dst, MTMP[0:r, m % 2, :], ALU.add).then_inc(merged, 1)

        X = mem(R + 7040, TILES, D)
        MT = mem(R + 12160, DC, TOK)
        H2 = mem(R + 22272, TILES, D)
        gain_ffn = mem(R + 5120, D)
        SQ8 = mem(R, D)
        turn8 = [take(n % 8) for n in range(2 * TILES)]
        proj8 = {(n, t): take(4 * n + t % (4 - n)) for n in range(2) for t in range(TILES)}
        part8 = [take(7) for _ in range(2)]
        PARTS8 = mem(R + 16512, 512)
        turn8b = [take(n % 8) for n in range(2 * TILES)]
        for n in range(2):
            last_use[f"wo{n}"] = proj8[n, PT]
        x8_in, gain8_in, m_ready, sq8, root8, inv8, h2_put = (
            sem("out_" + n) for n in ("x_in", "gain_in", "m_ready", "squares", "root", "inverse", "h2"))
        with nc.Block() as block:
            @block.sync
            def _(sp):
                sp.dma_start(X[:, 0:PT, :], ins["x_prompt"][0].rearrange("(t p) d -> p t d", p=P)).then_inc(x8_in, 16)
                sp.dma_start(X[0:NS, PT, :], ins["x_sample"].rearrange("b t d -> (b t) d")).then_inc(x8_in, 16)
                sp.dma_start(gain_ffn, ins["norm_ffn_g"].to_broadcast([P, D])).then_inc(gain8_in, 16)
                load_weights(sp, min(load_no["wo1"] + 4, len(order)))

            @block.tensor
            def _(pe):
                pe.wait_ge(consts_in, 16)
                transposes(pe, lambda t: M[:, t, :], turn8, consts_in, lambda t: 16)
                pe.wait_ge(m_ready, 2 * TILES)
                for n in range(2):
                    w = weights_there(pe, f"wo{n}")
                    sample_parts(pe, w, part8[n], MT)
                    for t in range(PT):
                        project(pe, w, t, proj8[n, t], MT)
                    sum_parts(pe, PARTS8, part8[n], proj8[n, PT])
                transposes(pe, lambda t: H2[:, t, :], turn8b, h2_put, lambda t: t + 1)

            @block.vector
            def _(dve):
                transposed_to(dve, MT, turn8)
                for u in turn8:
                    dve.wait_ge(bank_free[u[0]], u[1] + 1)
                dve.sem_inc(m_ready, 2 * TILES)
                dve.wait_ge(x8_in, 32)
                for n in range(2):
                    for t in range(TILES):
                        r = rows(t)
                        bank = reader_waits(dve, proj8[n, t])
                        x = X[0:r, t, n * 512:(n + 1) * 512]
                        freed(dve.tensor_tensor(x, x, bank[0:r, :], ALU.add), proj8[n, t])
                dve.wait_ge(gain8_in, 16)
                for t in range(TILES):
                    r = rows(t)
                    dve.wait_ge(root8, t + 1)
                    dve.reciprocal(stat[0:r, 8 + t:9 + t], stat2[0:r, t:t + 1]).then_inc(inv8, 1)
                    dve.wait_ge(inv8, t + 1)
                    dve.scalar_tensor_tensor(out=H2[0:r, t, :], in0=X[0:r, t, :], scalar=stat[0:r, 8 + t:9 + t],
                                             in1=gain_ffn[0:r, :], op0=ALU.mult, op1=ALU.mult).then_inc(h2_put, 1)
                transposed_to(dve, hT, turn8b)

            @block.scalar
            def _(act):
                for n in range(2):
                    keep_parts(act, PARTS8, part8[n], proj8[0, PT] if n else None)
                for t in range(TILES):
                    for n in range(2):
                        b, before = proj8[n, t]
                        act.wait_ge(bank_free[b], before + 1)
                    act.activation(SQ8[0:rows(t), :], X[0:rows(t), t, :], ACT.Square,
                                   accum_out=stat[0:rows(t), t:t + 1]).then_inc(sq8, 1)
                    act.wait_ge(sq8, t + 1)
                    act.activation(stat2[0:rows(t), t:t + 1], stat[0:rows(t), t:t + 1], ACT.Sqrt,
                                   bias=const("eps")[0:rows(t), :], scale=1.0 / D).then_inc(root8, 1)

        S_AT = R + 12160
        base = [OAT_AT]

        def small(*shape):
            n = 1
            for k in shape:
                n *= k
            if base[0] < R and base[0] + n > R:
                base[0] = SMALL2_AT
            base[0] += n
            assert base[0] <= R and (base[0] > OAT_AT or base[0] <= W_AT)
            return mem(base[0] - n, *shape)
        SC = small(2, 2, NKEY)
        SR = small(2, NKEY)
        MV, MIF, PF, E12 = small(2, TOPK), small(2, TOPK), small(2, TOPK), small(2, TOPK)
        MI = small(2, TOPK).bitcast(U32)
        PH = small(2, TOPK).bitcast(U32)
        CAND, CANDR, OH = small(TOPK, TOPK), small(TOPK * TOPK), small(2, TOPK, TOPK)
        TOP, EF, A2_, A3_, A4_, EX, R1_, AG = (small(TOPK) for _ in range(8))
        POS = small(TOPK).bitcast(U32)
        IDX = small(2, TOPK).bitcast(I32)
        G16, A16, W16 = small(2, TOPK), small(2, TOPK), small(2, TOPK)
        NEGM, SUM, RSUM = small(2), small(2), small(2)
        u_used, v_used, diag_put, x_added, idx_put, sc_put, hcur_put = (
            sem("peer_" + n) for n in ("u_used", "v_used", "diagonal_put", "x_added", "index_put", "scores_copied", "h2_copied"))
        negm_put, soft_put, exp_put, weights_put, cube_put, gelu_exp, tk_step, turn_taken, gl_step = (
            sem("peer_" + n) for n in ("negative_max", "top_put", "softmax_exp", "softmax", "gelu_argument", "gelu_exp",
                                       "topk_step", "turn_taken", "gelu_step"))
        TK_STEPS, GL_STEPS = 25, 7
        BETWEEN = 10
        topk_steps = set()

        def topk(dve, i, p):
            count = [0]

            def step(ins_, wait=True, apart=False):
                ins_.then_inc(tk_step, 1)
                count[0] += 1
                if wait:
                    dve.wait_ge(tk_step, i * TK_STEPS + count[0])
                    if apart:
                        dve.sem_inc(turn_taken, 1)
            dve.wait_ge(sc_put, i + 1)
            dve.sem_inc(turn_taken, 1)
            for c in range(2):
                step(dve.max(MV[:, c, 0:8], SC[:, p, c, :]), c == 1, True)
            for c in range(2):
                step(dve.max_index(MI[:, c, 0:8], MV[:, c, 0:8], SC[:, p, c, :]), False)
                step(dve.match_replace(SR[:, c, :], MV[:, c, 0:8], SC[:, p, c, :], GONE), c == 1, True)
            for c in range(2):
                step(dve.max(MV[:, c, 8:16], SR[:, c, :]), c == 1, True)
            for c in range(2):
                step(dve.max_index(MI[:, c, 8:16], MV[:, c, 8:16], SR[:, c, :]), False)
            step(dve.tensor_tensor(CAND, MV[:, 0, :].unsqueeze(2).to_broadcast([P, TOPK, TOPK]),
                                   MV[:, 1:2, :].to_broadcast([P, TOPK, TOPK]), ALU.add), apart=True)
            cand = CAND.rearrange("p a b -> p (a b)")
            step(dve.max(TOP[:, 0:8], cand), apart=True)
            step(dve.max_index(POS[:, 0:8], TOP[:, 0:8], cand), False)
            dve.tensor_scalar(NEGM[:, p:p + 1], TOP[:, 0:1], -1.0, None, ALU.mult).then_inc(negm_put, 1)
            step(dve.match_replace(CANDR, TOP[:, 0:8], cand, GONE), apart=True)
            step(dve.max(TOP[:, 8:16], CANDR), apart=True)
            dve.wait_ge(negm_put, i + 1)
            dve.sem_inc(soft_put, 1)
            step(dve.max_index(POS[:, 8:16], TOP[:, 8:16], CANDR), False)
            step(dve.tensor_copy(MIF, MI))
            step(dve.tensor_scalar(PH[:, 0, :], POS, 4, None, ALU.logical_shift_right), False)
            step(dve.tensor_scalar(PH[:, 1, :], POS, 15, None, ALU.bitwise_and))
            step(dve.tensor_copy(PF, PH))
            ranks = PF.rearrange("p c k -> p (c k)").unsqueeze(2).to_broadcast([P, 2 * TOPK, TOPK])
            iota = const("iota").unsqueeze(1).to_broadcast([P, 2 * TOPK, TOPK])
            step(dve.tensor_tensor(OH.rearrange("p c k j -> p (c k) j"), ranks, iota, ALU.is_equal))
            step(dve.tensor_tensor(OH, OH, MIF.unsqueeze(2).to_broadcast([P, 2, TOPK, TOPK]), ALU.mult))
            step(dve.tensor_reduce(E12.rearrange("p c k -> p (c k)"), OH.rearrange("p c k j -> p (c k) j"), AX.X, ALU.add))
            step(dve.scalar_tensor_tensor(out=EF, in0=E12[:, 0, :], scalar=float(NKEY), in1=E12[:, 1, :], op0=ALU.mult, op1=ALU.add))
            dve.wait_ge(exp_put, i + 1)
            step(dve.reciprocal(RSUM[:, p:p + 1], SUM[:, p:p + 1]))
            dve.tensor_scalar(G16[:, p, :], G16[:, p, :], RSUM[:, p:p + 1], None, ALU.mult).then_inc(weights_put, 1)
            topk_steps.add(count[0])

        def put_index(dve, p):
            dve.tensor_copy(IDX[:, p, :], EF).then_inc(idx_put, 1)

        def scores_copy(act, i, p):
            src = mem(S_AT, SLOTS * 2 * NKEY)[:, bass.ds(i * (2 * NKEY), 2 * NKEY)]
            act.activation(SC[:, p, :, :].rearrange("p c n -> p (c n)"), src, ACT.Copy).then_inc(sc_put, 1)

        def softmax_exp(act, i, p):
            act.wait_ge(soft_put, i + 1)
            act.activation(G16[:, p, :], TOP, ACT.Exp, bias=NEGM[:, p:p + 1],
                           accum_out=SUM[:, p:p + 1]).then_inc(exp_put, 1)

        RING = TOPK
        row_in = [sem(f"row_in{k}") for k in range(RING)]
        ring = [mem(W_AT + k * D, D) for k in range(RING)]
        assert W_AT + RING * D <= OAT_AT
        U_EARLY = range(4, 12)

        KEYS = mem(R, 2 * PEER_H, P)
        KEYT = mem(R + 2048, 2 * PEER_H, P)
        QP = mem(R + 4096, 2, SEQ)
        QPs = mem(R + 5120, 2 * PEER_H, NS)
        XS = mem(R + 5632, D)
        S = mem(S_AT, SLOTS, 2, NKEY)
        NB = 2 * PEER_H
        key_turn = [take(4 + k) for k in range(4)]
        q_use = [take(nb % 2) for nb in range(NB)]
        qs_use = [take(2 + nb % 2) for nb in range(NB)]
        s_use = [take(4 + nb % 2) for nb in range(NB)]
        ss_use = take(6)
        part9 = [take(7) for _ in range(4)]
        PARTS9 = mem(R + 20864, 512)
        for c in range(4):
            last_use[f"wq{c}"] = qs_use[4 * c + 3]
        keys9_in, xs_put = sem("peer_keys_in"), sem("peer_x_saved")
        with nc.Block() as block:
            @block.sync
            def _(sp):
                sp.dma_start(KEYS, ins["peer_sub_keys"][0].rearrange("h c n d -> n (h c) d")).then_inc(keys9_in, 16)
                load_weights(sp, len(order))

            @block.tensor
            def _(pe):
                pe.wait_ge(keys9_in, 16)
                for k in range(4):
                    bank = pe_claims(pe, key_turn[k])
                    for c in range(4):
                        last = pe.transpose(bank[:, c * P:(c + 1) * P], KEYS[:, 4 * k + c, :], ident)
                    filled(last, key_turn[k])

                def scores(nb):
                    h, c = nb // 2, nb % 2
                    pe.wait_ge(bank_free[qs_use[nb][0]], qs_use[nb][1] + 1)
                    pe.wait_ge(bank_free[q_use[nb][0]], q_use[nb][1] + 1)
                    if nb == 0:
                        for u in key_turn:
                            pe.wait_ge(bank_free[u[0]], u[1] + 1)
                    bank = pe_claims(pe, s_use[nb])
                    for t in range(PT):
                        last = pe.matmul(bank[:, t * P:(t + 1) * P], QP[:, nb % 2, cols(t)], KEYT[:, nb, :], start=True, stop=True)
                    filled(last, s_use[nb])
                    bank = pe_claims(pe, ss_use) if nb == 0 else ps[:, ss_use[0], :]
                    g, k = h // 2, (h % 2) * 2 + c
                    last = pe.matmul(bank[32 * g:32 * g + 32, k * P:(k + 1) * P], QPs[:, nb, :], KEYT[:, nb, :], start=True, stop=True)
                    if nb == NB - 1:
                        filled(last, ss_use)
                for nb in range(NB):
                    w = weights_there(pe, f"wq{nb // 4}")
                    if nb % 4 == 0:
                        sample_parts(pe, w, part9[nb // 4])
                    w = w[:, :, (nb % 4) * P:(nb % 4 + 1) * P]
                    bank = pe_claims(pe, q_use[nb])
                    for c in range(DC):
                        last = pe.matmul(bank[:, :], w[:, c, :], hT[:, c, 0:SEQ], start=(c == 0), stop=(c == DC - 1))
                    filled(last, q_use[nb])
                    b, before = part9[nb // 4]
                    pe.wait_ge(bank_free[b], before + 1)
                    bank = pe_claims(pe, qs_use[nb])
                    filled(pe.matmul(bank[:, 0:NS], PARTS9[:, (nb % 4) * P:(nb % 4 + 1) * P], const("gather4"),
                                     start=True, stop=True), qs_use[nb])
                    if nb:
                        scores(nb - 1)
                scores(NB - 1)

            @block.gpsimd
            def _(pool):
                pool.wait_ge(idx_put, 1)
                for k in U_EARLY:
                    for c in range(4):
                        lo = load_no[f"wq{c}"] % W_BUFS * W_SIZE
                        if lo <= k * D < lo + W_SIZE:
                            u = q_use[4 * c + 3]
                            pool.wait_ge(bank_full[u[0]], u[1] + 1)
                    pool.indirect_dma_start(ring[k], None, ins["peer_u"][0],
                                            bass.IndirectOffsetOnAxis(ap=IDX[:, 0, k:k + 1], axis=0)).then_inc(row_in[k], 16)

            @block.scalar
            def _(act):
                act.preload_act_table_set("natural_log_exp_and_others")
                for k in range(4):
                    bank = reader_waits(act, key_turn[k])
                    freed(act.activation(KEYT[:, 4 * k:4 * k + 4, :], bank.rearrange("p (c n) -> p c n", c=4), ACT.Copy), key_turn[k])
                for nb in range(NB):
                    if nb % 4 == 0:
                        keep_parts(act, PARTS9, part9[nb // 4], qs_use[nb - 1] if nb else None)
                    bank = reader_waits(act, q_use[nb])
                    if nb >= 2:
                        act.wait_ge(bank_full[s_use[nb - 2][0]], s_use[nb - 2][1] + 1)
                    freed(act.activation(QP[:, nb % 2, :], bank, ACT.Copy), q_use[nb])
                    bank = reader_waits(act, qs_use[nb])
                    freed(act.activation(QPs[:, nb, :], bank[:, 0:NS], ACT.Copy), qs_use[nb])
                    if nb == 6:
                        act.wait_ge(bank_free[s_use[2][0]], s_use[2][1] + 1)
                        act.wait_ge(bank_free[s_use[3][0]], s_use[3][1] + 1)
                        for i in range(2):
                            scores_copy(act, i, i)
                    if nb in (8, 10):
                        softmax_exp(act, nb // 2 - 4, nb // 2 - 4)

            @block.vector
            def _(dve):
                for g in range(1, 4):
                    dve.tensor_copy(H2[32 * g:32 * g + 32, PT, :], H2[0:NS, PT, :])
                dve.tensor_copy(XS[0:NS, :], X[0:NS, PT, :]).then_inc(xs_put, 1)
                dve.wait_ge(xs_put, 1)
                dve.memset(X[:, PT, :], 0.0).then_inc(xs_put, 1)
                for nb in range(NB):
                    h, c = nb // 2, nb % 2
                    bank = reader_waits(dve, s_use[nb])
                    dst = S[:, 0:PT * PEER_H, c, :].rearrange("p (t h) n -> p t h n", h=PEER_H)[:, :, h, :]
                    freed(dve.tensor_copy(dst, bank.rearrange("p (t n) -> p t n", t=PT)), s_use[nb])
                    if nb in (7, 9):
                        topk(dve, (nb - 7) // 2, (nb - 7) // 2)
                        put_index(dve, (nb - 7) // 2)
                bank = reader_waits(dve, ss_use)
                freed(dve.tensor_copy(S[:, PT * PEER_H:, :, :].rearrange("p a c n -> p (a c n)"), bank), ss_use)

        HCUR = mem(R, 2, D)
        u_rows, v_rows = ins["peer_u"][0], ins["peer_v"][0]

        WG = [mem(R + 12160, DC, 512), mem(R + 22272, DC, 512)]
        WE = mem(R + 2048, 2, D)
        XT, XTS = mem(R + 16256, DC, SEQ), mem(R + 28480, DC, NS)
        PB, PBT = mem(R + 20864, TILES, PLE), mem(R + 27392, 2, TOK)
        PARTS11 = [mem(R + 20864, 512), mem(R + 21376, 512)]
        GT = mem(R + 4608, 2, 512)
        DIAGS = 3
        DIAG = mem(R + 6656, DIAGS, P)
        V_SUM = 6
        SQ11 = mem(R + 4608, D)
        prompt_work = [(n, t) for n in range(2) for t in range(PT)]
        p_turn = [take(4 + t % 2) for t in range(TILES)]
        turn11 = [take(n % 4) for n in range(2 * PT)]
        gate_use = [take(m % 4) for m in range(2 * PT)]
        emb_use = [take(4 + m % 4) for m in range(2 * PT)]
        sum_use = [take(0), take(1)]
        turn_s = take(0)
        part11 = [take(3), take(2)]
        gate_s = [take(0), take(1)]
        emb_s = [take(4), take(5)]
        wg0_in, wg1_in = (sem("ple_" + n) for n in ("gate_weights_in0", "gate_weights_in1"))
        p_in, xsum, sq11, root11, inv11, gates_put, prod11, y_put = (
            sem("ple_" + n) for n in ("p_in", "sample_sum", "squares", "root", "inverse", "gate", "product", "y"))

        def slots_done(eng, n):
            eng.wait_ge(x_added, 2 * n + 2)
        with nc.Block() as block:
            @block.sync
            def _(sp):
                sp.dma_start(WE, ins["w_ple"][0].rearrange("(c p) n -> p c n", p=P)).then_inc(p_in, 16)
                sp.dma_start(PB[:, 0:PT, :], ins["p_prompt"][0, 0].rearrange("(t p) d -> p t d", p=P)).then_inc(p_in, 16)
                sp.dma_start(PB[0:NS, PT, :], ins["p_sample"][0].rearrange("b t d -> (b t) d")).then_inc(p_in, 16)
                w = ins["w_ple_gate"][0].rearrange("(c p) n -> p c n", p=P)
                sp.wait_ge(sc_put, PT * PEER_H)
                sp.dma_start(WG[0], w[:, :, 0:512]).then_inc(wg0_in, 16)
                sp.wait_ge(hcur_put, PT * PEER_H)
                sp.dma_start(WG[1], w[:, :, 512:D]).then_inc(wg1_in, 16)
                for m, (n, t) in enumerate(prompt_work + [(0, PT), (1, PT)]):
                    sp.wait_ge(y_put, m + 1)
                    dst = outs["y_prompt"][0, cols(t), :] if t < PT else outs["y_sample"].rearrange("b t d -> (b t) d")
                    store(sp, dst[:, n * 512:(n + 1) * 512], X[0:rows(t), t, n * 512:(n + 1) * 512])
                sp.wait_ge(stored, 16 * n_stored[0])

            @block.tensor
            def _(pe):
                def weigh_v(i, p):
                    pe.wait_ge(x_added, i * 2 + 2)
                    pe.sem_inc(turn_taken, 1)
                    for k in range(RING):
                        pe.wait_ge(row_in[k], i * 32 + 32)
                        pe.sem_inc(turn_taken, 1)
                        pe.wait_ge(diag_put, i * 16 + (k + 1))
                        pe.sem_inc(turn_taken, 1)
                        for n in range(2):
                            last = pe.matmul(ps[:, V_SUM + n, :], DIAG[:, k % DIAGS, :], ring[k][:, n * 512:(n + 1) * 512],
                                             start=(k == 0), stop=(k == RING - 1))
                        last.then_inc(v_used, 1)
                pe.wait_ge(p_in, 48)
                for t in range(TILES):
                    bank = pe_claims(pe, p_turn[t])
                    for c in range(2):
                        last = pe.transpose(bank[:, c * P:c * P + rows(t)], PB[0:rows(t), t, c * P:(c + 1) * P], ident[0:rows(t), 0:rows(t)])
                    filled(last, p_turn[t])
                with pe.Fori(0, PT * PEER_H // 2) as j:
                    for p in range(2):
                        weigh_v(j * 2 + p, p)
                for t in range(PT):
                    slots_done(pe, (t + 1) * PEER_H)
                    for half in range(2):
                        bank = pe_claims(pe, turn11[2 * t + half])
                        for c in range(4):
                            last = pe.transpose(bank[:, c * P:(c + 1) * P], X[:, t, (half * 4 + c) * P:(half * 4 + c + 1) * P], ident)
                        filled(last, turn11[2 * t + half])
                for u in turn11 + p_turn:
                    pe.wait_ge(bank_free[u[0]], u[1] + 1)
                for m, (n, t) in enumerate(prompt_work):
                    pe.wait_ge((wg0_in, wg1_in)[n], 16)
                    project(pe, WG[n], t, gate_use[m], XT)
                    project(pe, WE[:, :, n * 512:(n + 1) * 512], t, emb_use[m], PBT, 2)
                pe.wait_ge(v_used, RING * SLOTS)
                for n in range(2):
                    bank = pe_claims(pe, sum_use[n])
                    filled(pe.matmul(bank[0:NS, :], const("gather4"), X[:, PT, n * 512:(n + 1) * 512], start=True, stop=True), sum_use[n])
                for n in range(2):
                    project(pe, WE[:, :, n * 512:(n + 1) * 512], PT, emb_s[n], PBT, 2)
                pe.wait_ge(xsum, 2)
                bank = pe_claims(pe, turn_s)
                for c in range(DC):
                    last = pe.transpose(bank[:, c * NS:(c + 1) * NS], X[0:NS, PT, c * P:(c + 1) * P], ident[0:NS, 0:NS])
                filled(last, turn_s)
                pe.wait_ge(bank_free[turn_s[0]], turn_s[1] + 1)
                for n in range(2):
                    bank = pe_claims(pe, part11[n])
                    for c in range(DC):
                        g = c % 4
                        last = pe.matmul(bank[32 * g:32 * g + 32, :], XTS[:, c, :], WG[n][:, c, :], start=(c < 4), stop=(c >= 4),
                                         skip_group_check=True)
                    filled(last, part11[n])
                for n in range(2):
                    sum_parts(pe, PARTS11[n], part11[n], gate_s[n])

            @block.gpsimd
            def _(pool):
                def gather(table, p, i_needed, used, ks=range(RING)):
                    pool.wait_ge(idx_put, i_needed)
                    pool.sem_inc(turn_taken, 1)
                    for k in ks:
                        if k % 4 == 0 and used is not None:
                            pool.wait_ge(used[0], used[1] + (k + 4))
                            pool.sem_inc(turn_taken, 1)
                        pool.indirect_dma_start(ring[k], None, table, bass.IndirectOffsetOnAxis(ap=IDX[:, p, k:k + 1], axis=0)).then_inc(row_in[k], 16)

                def slot(i, p, last=False):
                    gather(v_rows, p, i + 1, (u_used, i * 16))
                    if not last:
                        gather(u_rows, 1 - p, i + 2, (v_used, i * 16))
                gather(u_rows, 0, 1, None, [k for k in range(RING) if k not in U_EARLY])
                with pool.Fori(0, PT * PEER_H // 2) as j:
                    for p in range(2):
                        slot(j * 2 + p, p)
                slot(PT * PEER_H, 0)
                slot(PT * PEER_H + 1, 1, last=True)

            @block.vector
            def _(dve):
                def gelu(i, p):
                    count = [0]

                    def step(ins_):
                        ins_.then_inc(gl_step, 1)
                        count[0] += 1
                        dve.wait_ge(gl_step, i * GL_STEPS + count[0])
                    a = A16[:, p, :]
                    dve.wait_ge(u_used, i * 16 + 16)
                    step(dve.tensor_tensor(A2_, a, a, ALU.mult))
                    step(dve.tensor_scalar(A3_, A2_, GELU_A, 1.0, ALU.mult, ALU.add))
                    step(dve.tensor_tensor(A2_, A3_, a, ALU.mult))
                    dve.tensor_scalar(A4_, A2_, -50.0, None, ALU.max).then_inc(cube_put, 1)
                    dve.wait_ge(weights_put, i + 1)
                    step(dve.tensor_tensor(AG, a, G16[:, p, :], ALU.mult))
                    dve.wait_ge(gelu_exp, i + 1)
                    step(dve.tensor_scalar(R1_, EX, 1.0, None, ALU.add))
                    step(dve.reciprocal(EX, R1_))
                    step(dve.tensor_tensor(W16[:, p, :], AG, EX, ALU.mult))
                    assert count[0] == GL_STEPS

                def use_v(i, p, x):
                    for k in range(RING):
                        dve.wait_ge(row_in[k], i * 32 + 32)
                        if k:
                            dve.wait_ge(v_used, i * 16 + k)
                        dve.scalar_tensor_tensor(out=x, in0=ring[k], scalar=W16[:, p, k:k + 1], in1=x, op0=ALU.mult,
                                                 op1=ALU.add).then_inc(v_used, 1)

                def add_v(i, x):
                    dve.wait_ge(v_used, i * 16 + 16)
                    dve.sem_inc(turn_taken, 1)
                    for n in range(2):
                        half = x[:, n * 512:(n + 1) * 512]
                        dve.scalar_tensor_tensor(out=half, in0=ps[:, V_SUM + n, :], scalar=1.0, in1=half, op0=ALU.mult,
                                                 op1=ALU.add).then_inc(x_added, 1)

                def use_u(i, p, between=lambda: None):
                    dve.wait_ge(hcur_put, i + 1)
                    for k in range(RING):
                        if k == BETWEEN:
                            between()
                        dve.wait_ge(row_in[k], i * 32 + 16)
                        dve.tensor_tensor_reduce(ring[k], ring[k], HCUR[:, p, :], 1.0, 0.0, ALU.mult, ALU.add,
                                                 A16[:, p, k:k + 1]).then_inc(u_used, 1)
                dve.sem_inc(x_added, 2)
                use_u(0, 0)
                with dve.Fori(0, PT * PEER_H // 2) as j:
                    x = mem(R + 7040, TILES * D)[:, bass.ds((j // 4) * D, D)]
                    for p in range(2):
                        i = j * 2 + p
                        gelu(i, p)
                        topk(dve, i + 2, p)

                        def between():
                            add_v(i, x)
                            put_index(dve, p)
                        use_u(i + 1, 1 - p, between)

                def embed(m, n, t, emb):
                    r = rows(t)
                    dve.wait_ge(gates_put, m + 1)
                    bank = reader_waits(dve, emb)
                    dve.tensor_tensor(GT[0:r, m % 2, :], bank[0:r, :], GT[0:r, m % 2, :], ALU.mult).then_inc(prod11, 1)
                    dve.wait_ge(prod11, m + 1)
                    dve.sem_inc(bank_free[emb[0]], 1)
                    x = X[0:r, t, n * 512:(n + 1) * 512]
                    dve.tensor_tensor(x, x, GT[0:r, m % 2, :], ALU.add).then_inc(y_put, 1)
                i = PT * PEER_H
                gelu(i, 0)
                dve.wait_ge(root11, 1)
                dve.reciprocal(stat[:, 8:8 + PT], stat2[:, 0:PT]).then_inc(inv11, 1)
                use_v(i, 0, X[:, PT, :])
                for m in range(PT):
                    embed(m, *prompt_work[m], emb_use[m])
                use_u(i + 1, 1)
                gelu(i + 1, 1)
                use_v(i + 1, 1, X[:, PT, :])
                assert topk_steps == {TK_STEPS}, topk_steps
                for n in range(2):
                    bank = reader_waits(dve, sum_use[n])
                    dve.wait_ge(bank_full[sum_use[1][0]], sum_use[1][1] + 1)
                    dve.tensor_tensor(X[0:NS, PT, n * 512:(n + 1) * 512], XS[0:NS, n * 512:(n + 1) * 512], bank[0:NS, :],
                                      ALU.add).then_inc(xsum, 1)
                    dve.wait_ge(xsum, n + 1)
                    dve.sem_inc(bank_free[sum_use[n][0]], 1)
                for m in range(PT, PT + 2):
                    embed(m, *prompt_work[m], emb_use[m])
                dve.wait_ge(root11, 2)
                dve.reciprocal(stat[0:NS, 8 + PT:9 + PT], stat2[0:NS, PT:PT + 1]).then_inc(inv11, 1)
                for m in range(PT + 2, 2 * PT):
                    embed(m, *prompt_work[m], emb_use[m])
                for n in range(2):
                    embed(2 * PT + n, n, PT, emb_s[n])

            @block.scalar
            def _(act):
                act.preload_act_table_set("natural_log_exp_and_others")

                def h2_copy(t, p):
                    act.activation(HCUR[:, p, :], mem(R + 22272, TILES * D)[:, bass.ds(t * D, D)], ACT.Copy).then_inc(hcur_put, 1)

                def gelu_part(i):
                    act.wait_ge(cube_put, i + 1)
                    act.activation(EX, A4_, ACT.Exp, scale=-2.0 * GELU_C).then_inc(gelu_exp, 1)

                def diagonals(i, p, ks):
                    for k in ks:
                        act.wait_ge(v_used, i * 16 + max(k - DIAGS + 1, 0))
                        act.activation(DIAG[:, k % DIAGS, :], ident, ACT.Copy, scale=W16[:, p, k:k + 1]).then_inc(diag_put, 1)
                h2_copy(0, 0)
                for t in range(TILES):
                    bank = reader_waits(act, p_turn[t])
                    freed(act.activation(PBT[:, :, cols(t)], bank[:, 0:2 * P].rearrange("p (c n) -> p c n", c=2)[:, :, 0:rows(t)], ACT.Copy), p_turn[t])
                with act.Fori(0, PT * PEER_H // 2) as j:
                    for p in range(2):
                        i = j * 2 + p
                        gelu_part(i)
                        act.wait_ge(gl_step, i * GL_STEPS + GL_STEPS)
                        diagonals(i, p, range(DIAGS))
                        scores_copy(act, i + 2, p)
                        h2_copy((j + p) // 4, 1 - p)
                        softmax_exp(act, i + 2, p)
                        diagonals(i, p, range(DIAGS, RING))

                def square_sum(t):
                    act.activation(SQ11[0:rows(t), :], X[0:rows(t), t, :], ACT.Square,
                                   accum_out=stat[0:rows(t), t:t + 1]).then_inc(sq11, 1)
                    act.wait_ge(sq11, t + 1)

                def gates(m, t, use):
                    r = rows(t)
                    act.wait_ge(inv11, 1 + t // PT)
                    if m >= 2:
                        act.wait_ge(y_put, m - 1)
                    bank = reader_waits(act, use)
                    act.activation(GT[0:r, m % 2, :], bank[0:r, :], ACT.Sigmoid, scale=stat[0:r, 8 + t:9 + t]).then_inc(gates_put, 1)
                    act.wait_ge(gates_put, m + 1)
                    act.sem_inc(bank_free[use[0]], 1)
                for t in range(PT):
                    slots_done(act, (t + 1) * PEER_H)
                    square_sum(t)
                    for half in range(2):
                        bank = reader_waits(act, turn11[2 * t + half])
                        for c in range(4):
                            last = act.activation(XT[:, half * 4 + c, cols(t)], bank[:, c * P:(c + 1) * P], ACT.Copy,
                                                  scale=ple_gain[:, half * 4 + c:half * 4 + c + 1])
                        freed(last, turn11[2 * t + half])
                act.activation(stat2[:, 0:PT], stat[:, 0:PT], ACT.Sqrt, bias=const("eps"), scale=1.0 / D).then_inc(root11, 1)
                act.preload_act_table_set("natural_log_exp_and_others")
                gelu_part(PT * PEER_H)
                h2_copy(PT, 1)
                for m in range(PT):
                    gates(m, prompt_work[m][1], gate_use[m])
                act.preload_act_table_set("natural_log_exp_and_others")
                gelu_part(PT * PEER_H + 1)
                for m in range(PT, PT + 2):
                    gates(m, prompt_work[m][1], gate_use[m])
                act.wait_ge(xsum, 2)
                act.wait_ge(y_put, PT + 2)
                square_sum(PT)
                act.activation(stat2[0:NS, PT:PT + 1], stat[0:NS, PT:PT + 1], ACT.Sqrt,
                               bias=const("eps")[0:NS, :], scale=1.0 / D).then_inc(root11, 1)
                bank = reader_waits(act, turn_s)
                for c in range(DC):
                    last = act.activation(XTS[:, c, :], bank[:, c * NS:(c + 1) * NS], ACT.Copy, scale=ple_gain[:, c:c + 1])
                freed(last, turn_s)
                for m in range(PT + 2, 2 * PT):
                    gates(m, prompt_work[m][1], gate_use[m])
                for n in range(2):
                    keep_parts(act, PARTS11[n], part11[n])
                for n in range(2):
                    gates(2 * PT + n, PT, gate_s[n])


_INS = ["x_prompt", "x_sample", "cache_k", "cache_v", "state_ret", "page_table", "p_prompt", "p_sample",
        "norm_mix_g", "w_in", "q_norm_g", "k_norm_g", "sb_bias", "ret_norm_g", "w_a_up", "w_b_up", "w_out",
        "norm_ffn_g", "peer_w_q", "peer_sub_keys", "peer_u", "peer_v", "norm_ple_g", "w_ple_gate", "w_ple"]
_OUTS = [("y_prompt", (1, SEQ, D)), ("y_sample", (DECB, DECT, D)),
         ("k_prompt", (1, 1, SEQ, H, HD)), ("v_prompt", (1, 1, SEQ, H, HD)), ("ret_prompt", (1, 1, RH, RK, RV)),
         ("k_sample", (1, DECB, DECT, H, HD)), ("v_sample", (1, DECB, DECT, H, HD)), ("ret_sample", (1, DECB, RH, RK, RV))]


def kernel(**inputs):
    import numpy as _np
    import concourse.bacc as _bacc
    from concourse import mybir as _mybir
    from concourse.bass_utils import run_bass_kernel_spmd as _run

    nc = _bacc.Bacc("TRN2", target_bir_lowering=False, num_devices=1)
    arrays, ins, outs = {}, {}, {}
    for name in _INS:
        a = _np.ascontiguousarray(inputs[name])
        arrays[f"in_{name}_dram"] = a
        ins[name] = nc.dram_tensor(f"in_{name}_dram", a.shape, _mybir.dt.from_np(a.dtype), kind="ExternalInput").ap()
    c = const_array()
    arrays["in_consts_dram"] = c
    consts = nc.dram_tensor("in_consts_dram", c.shape, _mybir.dt.from_np(c.dtype), kind="ExternalInput").ap()
    for name, shape in _OUTS:
        outs[name] = nc.dram_tensor(f"out_{name}_dram", shape, _mybir.dt.float32, kind="ExternalOutput").ap()
    bass_decoder_step(nc, ins, outs, consts)
    r = _run(nc, [arrays], core_ids=[0])
    return tuple(r.results[0][f"out_{name}_dram"] for name, _ in _OUTS)
```
